# Optimizing a Trainium2 kernel written in Bass

```python
import jax, jax.numpy as jnp
from jax import lax
import numpy as np

D_MODEL = 2048
BATCH = 1
SEQ = 512
DEPTH = 1

D_INNER = D_MODEL
GLA_WIDTH = D_INNER // 2
GLA_HEADS = 4
GLA_HEAD_V = GLA_WIDTH // GLA_HEADS
GLA_HEAD_K = GLA_HEAD_V // 2
GLA_KEY_WIDTH = GLA_HEADS * GLA_HEAD_K
GLA_LOWRANK = 16
GLA_TAU = 16.0
HGRN_WIDTH = D_INNER - GLA_WIDTH
HGRN_EXPAND = 128
HGRN_HEADS = HGRN_WIDTH // HGRN_EXPAND
HGRN_HEAD_V = HGRN_WIDTH // HGRN_HEADS
CHUNK = 64
EPS = 1e-6

SPLIT_SIZES = (GLA_KEY_WIDTH, GLA_KEY_WIDTH, GLA_WIDTH, GLA_WIDTH, GLA_LOWRANK,
               HGRN_WIDTH, HGRN_WIDTH, HGRN_WIDTH, HGRN_WIDTH)
D_PROJ = sum(SPLIT_SIZES)

kernel_name = "hymba_gla_hgrn2_parallel_layer"

def rmsnorm(x, g):
    x32 = x.astype(jnp.float32)
    y = x32 * lax.rsqrt(jnp.mean(x32 * x32, axis=-1, keepdims=True) + EPS)
    return (y * g.astype(jnp.float32)).astype(x.dtype)

def head_rmsnorm(o, g):
    B, T, H, dv = o.shape
    o32 = o.astype(jnp.float32)
    y = o32 * lax.rsqrt(jnp.mean(o32 * o32, axis=-1, keepdims=True) + EPS)
    return y.reshape(B, T, H * dv) * g.astype(jnp.float32)

def split_heads(a, n_heads):
    B, T, D = a.shape
    return a.reshape(B, T, n_heads, D // n_heads)

def chunked_gated_linear_attention(q, k, v, log_g, scale):
    B, T, H, dk = q.shape
    dv = v.shape[-1]
    n_chunks = T // CHUNK

    def to_chunks(a):
        a = a.astype(jnp.float32)
        return a.reshape(B, n_chunks, CHUNK, H, a.shape[-1]).transpose(1, 0, 3, 2, 4)

    qc = to_chunks(q) * scale
    kc, vc, gc = to_chunks(k), to_chunks(v), to_chunks(log_g)
    causal = jnp.tril(jnp.ones((CHUNK, CHUNK), dtype=bool))[:, :, None]

    def step(S, inp):
        q_, k_, v_, g_ = inp
        b = jnp.cumsum(g_, axis=-2)
        diff = b[..., :, None, :] - b[..., None, :, :]
        decay = jnp.exp(jnp.where(causal, diff, -jnp.inf))
        A = jnp.einsum('bhid,bhjd,bhijd->bhij', q_, k_, decay)
        o_intra = jnp.einsum('bhij,bhje->bhie', A, v_)
        o_inter = jnp.einsum('bhid,bhde->bhie', q_ * jnp.exp(b), S)
        b_last = b[..., -1:, :]
        k_dec = k_ * jnp.exp(b_last - b)
        S_new = jnp.exp(b_last)[..., 0, :, None] * S + jnp.einsum('bhjd,bhje->bhde', k_dec, v_)
        return S_new, o_intra + o_inter

    S0 = jnp.zeros((B, H, dk, dv), jnp.float32)
    _, out = lax.scan(step, S0, (qc, kc, vc, gc))
    return out.transpose(1, 0, 3, 2, 4).reshape(B, T, H, dv)

def setup_inputs(seed: int = 0) -> dict:
    key = jax.random.key(seed)
    ks = jax.random.split(key, 12)
    f32 = jnp.float32
    x = jax.random.normal(ks[0], (BATCH, SEQ, D_MODEL), f32)
    norm_w = 1.0 + 0.02 * jax.random.normal(ks[1], (DEPTH, D_MODEL), f32)
    w_in = jax.random.normal(ks[2], (DEPTH, D_MODEL, D_PROJ), f32) * D_MODEL ** -0.5
    gla_w_up = jax.random.normal(ks[3], (DEPTH, GLA_LOWRANK, GLA_KEY_WIDTH), f32) * GLA_LOWRANK ** -0.5
    gla_b_up = 0.1 * jax.random.normal(ks[4], (DEPTH, GLA_KEY_WIDTH), f32)
    gla_norm_w = 1.0 + 0.02 * jax.random.normal(ks[5], (DEPTH, GLA_WIDTH), f32)
    hgrn_lb_logits = 0.5 * jax.random.normal(ks[6], (DEPTH + 1, HGRN_WIDTH), f32)
    hgrn_norm_w = 1.0 + 0.02 * jax.random.normal(ks[7], (DEPTH, HGRN_WIDTH), f32)
    w_out = jax.random.normal(ks[8], (DEPTH, D_INNER, D_MODEL), f32) * D_INNER ** -0.5
    final_norm_w = 1.0 + 0.02 * jax.random.normal(ks[9], (D_MODEL,), f32)
    return {"x": x, "norm_w": norm_w, "w_in": w_in, "gla_w_up": gla_w_up,
            "gla_b_up": gla_b_up, "gla_norm_w": gla_norm_w,
            "hgrn_lb_logits": hgrn_lb_logits, "hgrn_norm_w": hgrn_norm_w,
            "w_out": w_out, "final_norm_w": final_norm_w}

def reference(x, norm_w, w_in, gla_w_up, gla_b_up, gla_norm_w, hgrn_lb_logits,
              hgrn_norm_w, w_out, final_norm_w):
    offsets = [int(o) for o in np.cumsum(SPLIT_SIZES)[:-1]]
    lb_all = jnp.cumsum(jax.nn.softmax(hgrn_lb_logits.astype(jnp.float32), axis=0), axis=0)
    for l in range(DEPTH):
        h = rmsnorm(x, norm_w[l])
        proj = h @ w_in[l]
        gq, gk, gv, gg, glr, hq, hf, hi, hg = jnp.split(proj, offsets, axis=-1)

        log_a = jax.nn.log_sigmoid((glr @ gla_w_up[l] + gla_b_up[l]).astype(jnp.float32)) / GLA_TAU
        o_a = chunked_gated_linear_attention(
            split_heads(gq, GLA_HEADS), split_heads(gk, GLA_HEADS),
            split_heads(gv, GLA_HEADS), split_heads(log_a, GLA_HEADS),
            GLA_HEAD_K ** -0.5)
        o_a = head_rmsnorm(o_a, gla_norm_w[l]) * jax.nn.silu(gg.astype(jnp.float32))

        lb = lb_all[l]
        f = lb + (1.0 - lb) * jax.nn.sigmoid(hf.astype(jnp.float32))
        o_b = chunked_gated_linear_attention(
            split_heads(hq, HGRN_HEADS), split_heads(1.0 - f, HGRN_HEADS),
            split_heads(hi, HGRN_HEADS), split_heads(jnp.log(f), HGRN_HEADS),
            HGRN_EXPAND ** -0.5)
        o_b = head_rmsnorm(o_b, hgrn_norm_w[l]) * jax.nn.silu(hg.astype(jnp.float32))

        mixed = jnp.concatenate([o_a, o_b], axis=-1).astype(x.dtype)
        x = x + mixed @ w_out[l]
    return rmsnorm(x, final_norm_w)


_drawn_inputs = setup_inputs


def setup_inputs(seed=0):
    import zlib

    import numpy as np

    out = dict(_drawn_inputs(seed))
    spreads = {}
    factors = {'gla_b_up': 3.589, 'gla_norm_w': 7.445, 'hgrn_norm_w': 7.912, 'final_norm_w': 2.786}
    for name, (base, spread) in spreads.items():
        noise = np.random.default_rng([zlib.crc32(name.encode()), seed]).standard_normal(out[name].shape)
        drawn = base * np.exp(spread * noise) if base else spread * noise
        out[name] = __import__('jax').numpy.asarray(drawn.astype(out[name].dtype))
    for name, factor in factors.items():
        out[name] = (out[name] * factor).astype(out[name].dtype)
    return out
```

```python
from contextlib import ExitStack

import concourse.bass as bass
from concourse import mybir

ALU = mybir.AluOpType
ACT = mybir.ActivationFunctionType
F32 = mybir.dt.float32
F32R = mybir.dt.float32r
BF16 = mybir.dt.bfloat16
U8 = mybir.dt.uint8

P = 128
T = 512
D = 2048
NT = T // P
KT = D // P
GLA_H, HG_H = 4, 8
LOWRANK = 16
TAU = 16.0
EPS = 1e-6
SCALE = float(P) ** -0.5
GW = 512
PK = 2
NP = KT // PK
RAW, SPL = 2, 4
LEAD = 3

C_GQ, C_GK, C_GV, C_GG = 0, 512, 1024, 2048
C_LR = 3072
C_HQ, C_HF, C_HI, C_HG = 3088, 4112, 5136, 6160
G_V, G_C, G_D, G_E, G_F, G_END = 2, 4, 8, 10, 14, 18

LV = [4, 8, 16, 32, 64]
NL = 1 + len(LV)
NEXP = 3 + len(LV) + 1
NARG = 3 + len(LV)
R_LOG, R_BUP, R_GNW, R_HNW, R_END = 0, 16, 20, 28, 36
T_HQ, T_HF, T_GA = 8, 16, 20
LN_SHIFT = 20
G_MIN = -50.0
LB_MIN = 2.0 ** -60


EXL = [None, 2, 3, 0, 1, 3]
LN2 = 0.6931471805599453
A_C, A_E, V_C, V_E = 26, 28, 86, 86


class Steps:

    def __init__(self, eng, sem, i=0, per=0):
        self.eng, self.sem, self.i, self.per, self.n = eng, sem, i, per, 0

    def __call__(self, ins):
        self.n += 1
        ins.then_inc(self.sem, 1)
        self.eng.wait_ge(self.sem, self.i * self.per + self.n)
        return ins

    def check(self):
        assert self.n == self.per, (self.sem, self.n)


def hymba_kernel(nc, x, norm_w, w_in, gla_w_up, gla_b_up, gla_norm_w, lb_logits, hgrn_norm_w, w_out,
                 final_norm_w, out):
    with ExitStack() as ctx:
        def sb(name, shape, dt=F32):
            return ctx.enter_context(nc.sbuf_tensor(name, shape, dt))

        def ps(name):
            return ctx.enter_context(nc.psum_tensor(name, [P, 512], F32))

        def sem(name):
            return ctx.enter_context(nc.semaphore(name))

        h_hi = sb("h_hi", [P, KT, T], F32R)
        h_lo = sb("h_lo", [P, KT, T], F32R)
        raw = sb("raw", [P, RAW, PK, GW])
        w_hi = sb("w_hi", [P, SPL, PK, GW], F32R)
        w_lo = sb("w_lo", [P, SPL, PK, GW], F32R)
        feat = sb("feat", [P, 24, T])
        val = sb("val", [P, NT, 1024])
        reset = sb("reset", [P, T], BF16)
        bcum = sb("bcum", [P, T])
        gdec = sb("gdec", [P, T])
        ex = [sb(f"ex{i}", [P, T]) for i in range(4)]
        kl = [sb(f"kl{i}", [P, T]) for i in range(2)]
        ql = [sb("ql0", [P, T]), sb("ql1", [P, T // 2])]
        kd = sb("kd", [P, 3 * P])
        kdT = sb("kdT", [P, 3 * P])
        qe = sb("qe", [P, 3 * P])
        att = sb("att", [P, T])
        state = sb("state", [P, 3 * P])
        vst = [sb(f"vst{i}", [P, NT, P]) for i in range(2)]
        sq = sb("sq", [P, T])
        gate = sb("gate", [P, T])
        mask0 = sb("mask0", [P, T], U8)
        maskl = [sb(f"mask{s}", [P, T // 2], U8) for s in LV]
        ones = sb("ones", [P, P])
        ident = sb("ident", [P, P])
        par = sb("par", [P, R_END])
        lb = sb("lb", [P, HG_H])
        oml = sb("oml", [P, HG_H])
        noml = sb("noml", [P, HG_H])
        cst = sb("cst", [P, 4])
        lbt = sb("lbt", [P, 2 * HG_H])
        mid = sb("mid", [P, P])
        dec = sb("dec", [P, 2])
        rsum = sb("rsum", [P, NT])
        rs = sb("rs", [P, 4 * NT])

        main = [ps(f"main{c}") for c in range(4)]
        sc = [ps("sc0"), ps("sc1")]
        po = ps("po")
        st = ps("st")

        xin = feat[:, 0:16, :].rearrange("p (t a) n -> p t (a n)", t=NT)
        nwb = feat[:, 16:20, :].rearrange("p a n -> p (a n)")
        junk = feat[:, 20:24, :].rearrange("p a n -> p (a n)")
        lr_raw = bcum[:, 0:KT * LOWRANK].rearrange("p (k r) -> p k r", k=KT)
        lr = ex[0]
        wup = ex[1]
        prow = gate
        y = [val[:, 0:2, :].rearrange("p a n -> p (a n)"), val[:, 2:4, :].rearrange("p a n -> p (a n)"),
             feat[:, 16:20, :].rearrange("p a n -> p (a n)"), feat[:, 20:24, :].rearrange("p a n -> p (a n)")]
        fnb = feat[:, 0:4, :].rearrange("p a n -> p (a n)")
        fjunk = feat[:, 4:5, :].rearrange("p a n -> p (a n)")

        def lrw(w):
            return w[:, SPL - 1, :, :].rearrange("p a (b m) -> p (a b) m", m=P)

        x_in = [sem(f"x_in{t}") for t in range(NT)]
        nw_in = sem("nw_in")
        par_in = sem("par_in")
        lr_in = sem("lr_in")
        up_in = sem("up_in")
        raw_in = [sem(f"raw_in{s}") for s in range(RAW)]
        x2_in = sem("x2_in")
        fn_in = sem("fn_in")
        out_done = sem("out_done")
        consts = sem("consts")
        a_step, v_step, p_step = sem("a_step"), sem("v_step"), sem("p_step")
        a_c, v_c = sem("a_c"), sem("v_c")
        a_e, v_e = sem("a_e"), sem("v_e")
        a_f = sem("a_f")
        lrw_zero, lb_arg, lb_ok, z_ok, k_ok, gate_used, mix_ok, ysum, yrt = (sem(n) for n in (
            "lrw_zero", "lb_arg", "lb_ok", "z_ok", "k_ok", "gate_used", "mix_ok", "ysum", "yrt"))
        sc_seen = sem("sc_seen")
        xss = sem("xss")
        xn_ok = sem("xn_ok")
        xt_ps, xt_hi, xt_lo = sem("xt_ps"), sem("xt_hi"), sem("xt_lo")
        par_ps, par_ok = sem("par_ps"), sem("par_ok")
        lb_e = sem("lb_e")
        lrw_hi, lrw_ok, lr_ps, lr_ok, z_ps, z_abs = (sem(n) for n in ("lrw_hi", "lrw_ok", "lr_ps", "lr_ok", "z_ps", "z_abs"))
        hi_ok, lo_ok, piece_done = sem("hi_ok"), sem("lo_ok"), sem("piece_done")
        full = sem("full")
        free = [sem(f"free{c}") for c in range(4)]
        g_ok = sem("g_ok")
        gate_ok = sem("gate_ok")
        arg_ok, exp_ok, kd_ok = sem("arg_ok"), sem("exp_ok"), sem("kd_ok")
        kT_ps, kT_ok, v_ok = sem("kT_ps"), sem("kT_ok"), sem("v_ok")
        lvl_ok, sc_ps, sc_ok = sem("lvl_ok"), sem("sc_ps"), sem("sc_ok")
        u_ps, s_ok, o_ps, sq_ok, ms_ps, rstd_ok = (sem(n) for n in ("u_ps", "s_ok", "o_ps", "sq_ok", "ms_ps", "rstd_ok"))
        mix_hi, mix_lo = sem("mix_hi"), sem("mix_lo")
        yss, yn = sem("yss"), sem("yn")

        def wait_bank(eng, G, c):
            if c < 3:
                eng.wait_ge(full, G * 3 + (c + 1))
            else:
                eng.wait_ge(piece_done, G * NP + NP)

        block = ctx.enter_context(nc.Block())

        @block.sync
        def _(sp):
            def group(src, col, G, pieces=range(NP)):
                for p in pieces:
                    n = NP * G + p
                    s = p % RAW
                    if not (isinstance(n, int) and n < RAW):
                        sp.wait_ge(lo_ok, n - RAW + 1)
                    rows = src[p * PK * P:(p + 1) * PK * P, bass.ds(col, GW)]
                    sp.dma_start(raw[:, s, :, :], rows.rearrange("(k p) n -> p k n", p=P)).then_inc(raw_in[s], 16)

            sp.dma_start(xin[:, 0, :], x[0:P, :]).then_inc(x_in[0], 16)
            sp.dma_start(nwb, norm_w.partition_broadcast(P)).then_inc(nw_in, 16)
            for t in range(1, NT):
                sp.dma_start(xin[:, t, :], x[t * P:(t + 1) * P, :]).then_inc(x_in[t], 16)
            sp.dma_start(prow[R_LOG:R_BUP, 0:P], lb_logits).then_inc(par_in, 16)
            sp.dma_start(prow[R_BUP:R_GNW, 0:P], gla_b_up).then_inc(par_in, 16)
            sp.dma_start(prow[R_GNW:R_HNW, 0:P], gla_norm_w).then_inc(par_in, 16)
            sp.dma_start(prow[R_HNW:R_END, 0:P], hgrn_norm_w).then_inc(par_in, 16)
            sp.dma_start(lr_raw, w_in[:, C_LR:C_LR + LOWRANK].rearrange("(k p) r -> p k r", p=P)).then_inc(lr_in, 16)
            for a in range(2):
                sp.dma_start(wup[a * LOWRANK:(a + 1) * LOWRANK, :], gla_w_up).then_inc(up_in, 16)
            for G in range(G_V):
                group(w_in, C_GQ + GW * G, G)
            with sp.Fori(0, 2) as i:
                group(w_in, i * GW + C_GV, i + G_V)
            with sp.Fori(0, 2) as i:
                group(w_in, i * GW + C_HQ, i * 2 + G_C)
                group(w_in, i * GW + C_HF, i * 2 + (G_C + 1))
            with sp.Fori(0, 2) as i:
                group(w_in, i * GW + C_HI, i + G_D)
            with sp.Fori(0, 2) as i:
                group(w_in, i * GW + C_GG, i + G_E)
            with sp.Fori(0, 2) as i:
                group(w_in, i * GW + C_HG, i + (G_E + 2))
            group(w_out, 0, G_F, range(LEAD + 1))
            sp.wait_ge(mix_lo, KT)
            for t in range(NT):
                sp.dma_start(y[t], x[t * P:(t + 1) * P, :]).then_inc(x2_in, 16)
            sp.dma_start(fnb, final_norm_w.partition_broadcast(P)).then_inc(fn_in, 16)
            group(w_out, 0, G_F, range(LEAD + 1, NP))
            with sp.Fori(0, 3) as i:
                group(w_out, i * GW + GW, i + (G_F + 1))
            for t in range(NT):
                sp.wait_ge(yn, t + 1)
                sp.dma_start(out[t * P:(t + 1) * P, :], y[t]).then_inc(out_done, 16)
            sp.wait_ge(out_done, 16 * NT)

        @block.gpsimd
        def _(pool):
            n = [0]

            def step(ins):
                n[0] += 1
                ins.then_inc(p_step, 1)
                pool.wait_ge(p_step, n[0])

            step(pool.memset(ones[:, :], 1.0))
            step(pool.memset(ident[:, :], 0.0))
            step(pool.affine_select(out=ident[:, :], in_=ident[:, :], compare_op=ALU.not_equal, fill=1.0, base=0,
                                    pattern=[[-1, P]], channel_multiplier=1))
            pool.sem_inc(consts, 1)
            step(pool.memset(reset[:, :], 1.0))
            step(pool.memset(reset[:, :].rearrange("p (c n) -> p c n", c=NT)[:, :, 0:1], 0.0))
            m = gdec
            step(pool.memset(m[:, :], 1.0))
            step(pool.affine_select(out=m[:, :], in_=m[:, :], compare_op=ALU.is_ge, fill=0.0, base=0,
                                    pattern=[[0, NT], [-4, P // 4], [0, 4]], channel_multiplier=1))
            step(pool.affine_select(out=m[:, :], in_=m[:, :], compare_op=ALU.is_ge, fill=0.0, base=0,
                                    pattern=[[0, NT], [4, P // 4], [1, 4]], channel_multiplier=-1))
            step(pool.tensor_copy(mask0[:, :], m[:, :]))
            for s, mk in zip(LV, maskl):
                m = gdec[:, 0:T // 2]
                step(pool.memset(m, 1.0))
                step(pool.affine_select(out=m, in_=m, compare_op=ALU.is_ge, fill=0.0, base=0,
                                        pattern=[[0, NT], [-2 * s, P // (2 * s)], [0, s]], channel_multiplier=1))
                step(pool.affine_select(out=m, in_=m, compare_op=ALU.is_ge, fill=0.0, base=s - 1,
                                        pattern=[[0, NT], [2 * s, P // (2 * s)], [0, s]], channel_multiplier=-1))
                step(pool.tensor_copy(mk[:, :], m))
            step(pool.memset(att[:, :], 0.0))
            pool.sem_inc(consts, 1)

        @block.tensor
        def _(pe):
            def group(G, tokens_stationary, tasks=None):
                tasks = tasks or {}
                for p in range(NP):
                    pe.wait_ge(lo_ok, G * NP + (p + 1))
                    s = p % SPL
                    for c in range(4):
                        if p == 0 and not (isinstance(G, int) and G == 0):
                            pe.wait_ge(free[c], G * 1)
                        for kk in range(PK):
                            k = p * PK + kk
                            cs = slice(c * P, (c + 1) * P)
                            if tokens_stationary:
                                pairs = [(h_hi[:, k, cs], w_hi[:, s, kk, :]), (h_hi[:, k, cs], w_lo[:, s, kk, :]),
                                         (h_lo[:, k, cs], w_hi[:, s, kk, :])]
                            else:
                                pairs = [(w_hi[:, s, kk, cs], h_hi[:, k, :]), (w_hi[:, s, kk, cs], h_lo[:, k, :]),
                                         (w_lo[:, s, kk, cs], h_hi[:, k, :])]
                            for j, (a, b) in enumerate(pairs):
                                mm = pe.matmul(main[c][:, :], a, b, start=(k == 0 and j == 0),
                                               stop=(k == KT - 1 and j == 2))
                        if c == 3:
                            mm.then_inc(piece_done, 1)
                        elif p == NP - 1:
                            mm.then_inc(full, 1)
                        for f in tasks.get(4 * p + c, ()):
                            f()

            def head_tasks(H, X, nx, at):
                def transposes():
                    pe.wait_ge(kd_ok, H + 1)
                    for c in range(3):
                        mm = pe.transpose(st[:, c * P:(c + 1) * P], kd[:, c * P:(c + 1) * P], ident[:, :])
                    mm.then_inc(kT_ps, 1)

                def level(l):
                    def f():
                        pe.wait_ge(lvl_ok, H * NL + (l + 1))
                        if l >= 2:
                            pe.wait_ge(sc_ok, H * NL + (l - 1))
                        w = P if l == 0 else P // 2
                        for c in range(NT):
                            mm = pe.matmul(sc[l % 2][:, c * w:(c + 1) * w], kl[l % 2][:, c * P:(c + 1) * P],
                                           ql[l % 2][:, c * w:(c + 1) * w], start=True, stop=True)
                        mm.then_inc(sc_ps, 1)
                    return f

                def update(xx):
                    def f():
                        if xx == 0:
                            pe.wait_ge(kT_ok, H + 1)
                        pe.wait_ge(v_ok, X + (xx + 1))
                        for c in range(3):
                            mm = pe.matmul(st[:, c * P:(c + 1) * P], kdT[:, c * P:(c + 1) * P], vst[vs(xx)][:, c, :],
                                           start=True, stop=True)
                        mm.then_inc(u_ps, 1)
                    return f

                def outputs(xx):
                    def f():
                        pe.wait_ge(sc_ok, H * NL + NL)
                        pe.wait_ge(s_ok, X + (xx + 1))
                        for c in range(NT):
                            cs = slice(c * P, (c + 1) * P)
                            mm = pe.matmul(po[:, cs], vst[vs(xx)][:, c, :], att[:, cs], start=True, stop=(c == 0))
                            if c:
                                mm = pe.matmul(po[:, cs], state[:, (c - 1) * P:c * P], qe[:, (c - 1) * P:c * P],
                                               start=False, stop=True)
                        mm.then_inc(o_ps, 1)
                    return f

                def meansq(xx):
                    def f():
                        pe.wait_ge(sq_ok, X + (xx + 1))
                        mm = pe.matmul(sc[0][:, :], ones[:, :], sq[:, :], start=(xx == 0), stop=(xx == nx - 1))
                        if xx == nx - 1:
                            mm.then_inc(ms_ps, 1)
                    return f

                def vs(xx):
                    return xx if nx == 2 else at["slot"]

                todo = {}
                todo.setdefault(at["T"], []).append(transposes)
                for l in range(NL):
                    todo.setdefault(at["L"][l], []).append(level(l))
                for xx in range(nx):
                    todo.setdefault(at["U"][xx], []).append(update(xx))
                    todo.setdefault(at["O"][xx], []).append(outputs(xx))
                    todo.setdefault(at["M"][xx], []).append(meansq(xx))
                return todo

            pe.wait_ge(consts, 1)
            for t in range(NT):
                pe.wait_ge(xn_ok, t + 1)
                for j in range(4):
                    if t:
                        pe.wait_ge(xt_lo, 4 * (t - 1) + j + 1)
                    for k in range(4 * j, 4 * j + 4):
                        mm = pe.transpose(main[j][:, (k % 4) * P:(k % 4 + 1) * P], xin[:, t, k * P:(k + 1) * P], ident[:, :])
                    mm.then_inc(xt_ps, 1)
            pe.wait_ge(par_in, 64)
            pe.transpose(po[:, 0:R_END], prow[0:R_END, 0:P], ident[0:R_END, 0:R_END]).then_inc(par_ps, 1)
            pe.wait_ge(lrw_ok, 1)
            pe.wait_ge(xt_lo, 4 * NT)
            for k in range(KT):
                w = lrw(w_hi if k < 8 else w_lo)[:, k % 8, :]
                pe.matmul(st[:, :], w, h_hi[:, k, :], start=(k == 0), stop=False)
                mm = pe.matmul(st[:, :], w, h_lo[:, k, :], start=False, stop=(k == KT - 1))
            mm.then_inc(lr_ps, 1)

            def decay_inputs():
                pe.wait_ge(lr_ok, 1)
                pe.wait_ge(up_in, 32)
                for h, bank in enumerate((sc[0], sc[1], po, st)):
                    mm = pe.matmul(bank[:, :], wup[0:2 * LOWRANK, h * P:(h + 1) * P], lr[0:2 * LOWRANK, :],
                                   start=True, stop=True)
                    mm.then_inc(z_ps, 1)

            group(0, False, {2: [decay_inputs]})
            group(1, False)
            with pe.Fori(0, 2) as i:
                group(i + G_V, True)
            gla_at = dict(T=7, L=[9, 11, 12, 14, 15, 17], U=[13, 22], O=[19, 24], M=[21, 26])
            with pe.Fori(0, 2) as i:
                for a in range(2):
                    H = i * 2 + a
                    group(i * 2 + (G_C + a), False, head_tasks(H, H * 2, 2, gla_at))

            def hg_at(u):
                z = 16 * u
                return dict(slot=u, T=z + 3, L=[z + q for q in (4, 5, 7, 8, 10, 11)], U=[z + 6], O=[z + 12], M=[z + 13])

            def hg_pair(m):
                return head_tasks(m + GLA_H, m + 8, 1, hg_at(0)) | head_tasks(m + (GLA_H + 1), m + 9, 1, hg_at(1))

            group(G_D, True)
            group(G_D + 1, True, hg_pair(0))
            with pe.Fori(0, 3) as i:
                group(i + G_E, False, hg_pair(i * 2 + 2))
            group(G_E + 3, False)
            pe.wait_ge(mix_lo, KT)
            with pe.Fori(0, 4) as i:
                group(i + G_F, True)

        @block.scalar
        def _(act):
            step = Steps(act, a_step)

            def split(G, p):
                q = p + LEAD
                if isinstance(G, int) and G * NP + q >= G_END * NP:
                    return
                act.wait_ge(raw_in[q % RAW], G * (NP // RAW * 16) + 16 * (q // RAW + 1))
                if not (isinstance(G, int) and G * NP + q < SPL):
                    act.wait_ge(piece_done, G * NP + (q - SPL + 1))
                act.activation(w_hi[:, q % SPL, :, :], raw[:, q % RAW, :, :], ACT.Copy).then_inc(hi_ok, 1)

            def group(G, tasks, take):
                for p in range(NP):
                    split(G, p)
                    for f in tasks.get(p, ()):
                        f()
                for c in range(4):
                    wait_bank(act, G, c)
                    take(c)

            def head(H, X, nx, step, slot, slots, q_tile):
                def e(n_arg, dst, src, scale=1.0):
                    act.wait_ge(arg_ok, H * NARG + n_arg)
                    step(act.activation(dst, src, ACT.Exp, scale=scale))
                    act.sem_inc(exp_ok, 1)

                def decay():
                    m = X - 8
                    r = feat[:, m + T_HF, :]
                    step(act.activation(gdec[:, :], r, ACT.Ln, bias=lb[:, bass.ds(m, 1)], scale=oml[:, bass.ds(m, 1)]))
                    act.sem_inc(g_ok, 1)
                    step(act.activation(r, r, ACT.Identity, bias=oml[:, bass.ds(m, 1)], scale=noml[:, bass.ds(m, 1)]))
                    act.sem_inc(k_ok, 1)

                def first():
                    if nx == 1:
                        decay()
                    e(2, ex[2][:, 0:3 * P], ex[2][:, 0:3 * P])
                    e(2, ex[3][:, 0:3 * P], bcum[:, P:T])
                    e(3, ex[1][:, :], ex[0][:, :], -1.0)
                    e(3, ex[0][:, :], ex[0][:, :])
                    for xx in range(nx):
                        col = (X + xx) * P if nx == 2 else (X - 8) * P
                        act.activation(vst[vslot(xx)][:, :, :], val[:, :, bass.ds(col, P)], ACT.Copy).then_inc(v_ok, 1)

                def level(l):
                    e(3 + l, ex[EXL[l]][:, :], ex[EXL[l]][:, :])

                def vslot(xx):
                    return xx if nx == 2 else slot

                def second():
                    level(1)
                    act.wait_ge(kT_ps, H + 1)
                    act.activation(kdT[:, :], st[:, 0:3 * P], ACT.Copy).then_inc(kT_ok, 1)
                    level(2)

                def third():
                    for l in (3, 4, 5):
                        level(l)

                def take(xx):
                    def f():
                        act.wait_ge(o_ps, X + (xx + 1))
                        act.activation(feat[:, q_tile + xx, :], po[:, :], ACT.Copy)
                        step(act.activation(sq[:, :], po[:, :], ACT.Square))
                        act.sem_inc(sq_ok, 1)
                    return f

                def rstd():
                    act.wait_ge(ms_ps, H + 1)
                    step(act.activation(sq[:, :], sc[0][:, :], ACT.Ln, bias=cst[:, 0:1],
                                        scale=2.0 ** -LN_SHIFT / (P * nx)))
                    step(act.activation(sq[:, :], sq[:, :], ACT.Exp, bias=cst[:, 1:2], scale=-0.5))
                    act.sem_inc(rstd_ok, 1)

                todo = {}
                for name, f in (("first", first), ("second", second), ("third", third), ("take0", take(0)),
                                ("take1", take(1)), ("rstd", rstd)):
                    if name in slots:
                        todo.setdefault(slots[name], []).append(f)
                return todo

            act.wait_ge(consts, 3)

            def squares(t):
                act.wait_ge(x_in[t], 16)
                step(act.activation(junk, xin[:, t, :], ACT.Square, accum_out=rs[:, t:t + 1]))
                step(act.activation(rs[:, t:t + 1], rs[:, t:t + 1], ACT.Sqrt, bias=cst[:, 2:3], scale=1.0 / D))
                act.sem_inc(xss, 1)

            def highs(t):
                for j in range(4):
                    act.wait_ge(xt_ps, 4 * t + j + 1)
                    act.activation(h_hi[:, 4 * j:4 * j + 4, t * P:(t + 1) * P],
                                   main[j][:, :].rearrange("p (a n) -> p a n", a=4), ACT.Copy).then_inc(xt_hi, 1)

            squares(0)
            squares(1)
            highs(0)
            squares(2)
            highs(1)
            squares(3)
            highs(2)
            act.wait_ge(lr_in, 16)
            act.wait_ge(lrw_zero, 1)
            for a, w in enumerate((w_hi, w_lo)):
                step(act.activation(lrw(w)[:, :, 0:LOWRANK], lr_raw[:, 8 * a:8 * a + 8, :], ACT.Copy))
            act.sem_inc(lrw_hi, 1)
            for p in range(-LEAD, 0):
                split(0, p)
            highs(3)
            act.wait_ge(lb_arg, 1)
            step(act.activation(lbt[:, :], lbt[:, :], ACT.Exp))
            act.sem_inc(lb_e, 1)
            act.wait_ge(lr_ps, 1)
            act.activation(lr[0:2 * LOWRANK, :], st[0:2 * LOWRANK, :], ACT.Copy).then_inc(lr_ok, 1)

            def decays():
                for h, bank in enumerate((sc[0], sc[1], po, st)):
                    act.wait_ge(z_ps, h + 1)
                    if h >= 2:
                        act.wait_ge(z_ok, h - 1)
                    t = ex[2 + h % 2][:, :]
                    step(act.activation(t, bank[:, :], ACT.Abs, bias=par[:, R_BUP + h:R_BUP + h + 1]))
                    step(act.activation(t, t, ACT.Exp, scale=-1.0))
                    step(act.activation(t, t, ACT.Ln, bias=cst[:, 3:4]))
                    act.sem_inc(z_abs, 1)

            def store(tile, scale=1.0, func=ACT.Copy):
                def f(c):
                    act.activation(feat[:, tile(c), :], main[c][:, :], func, scale=scale).then_inc(free[c], 1)
                return f

            group(0, {1: [decays]}, store(lambda c: 2 * c, SCALE))
            group(1, {}, store(lambda c: 2 * c + 1))
            with act.Fori(0, 2) as i:
                group(i + G_V, {}, lambda c: None)
            gla = dict(first=0, second=1, third=2, take0=4, take1=5, rstd=6)
            with act.Fori(0, 2) as i:
                stp = Steps(act, a_c, i, A_C)
                for a in range(2):
                    H = i * 2 + a
                    group(i * 2 + (G_C + a), head(H, H * 2, 2, stp, 0, gla, H * 2),
                          store(lambda c: i * 4 + (T_HQ + c), SCALE) if a == 0 else
                          store(lambda c: i * 4 + (T_HF + c), 1.0, ACT.Sigmoid))
                stp.check()

            def hg_pair(m, stp):
                todo = {}
                for u in range(2):
                    for q, fs in head(m + (GLA_H + u), m + (8 + u), 1, stp, u,
                                      dict(first=4 * u, second=4 * u + 1, third=4 * u + 2, take0=4 * u + 3,
                                           rstd=4 * u + 3), m + (8 + u)).items():
                        todo.setdefault(q, []).extend(fs)
                return todo

            def sigmoids(e):
                def f(c):
                    if c:
                        act.wait_ge(gate_used, e * 4 + c)
                    act.activation(gate[:, :], main[c][:, :], ACT.Sigmoid).then_inc(gate_ok, 1)
                return f

            group(G_D, {}, lambda c: None)
            group(G_D + 1, hg_pair(0, step), lambda c: None)
            with act.Fori(0, 3) as i:
                stp = Steps(act, a_e, i, A_E)
                group(i + G_E, hg_pair(i * 2 + 2, stp), sigmoids(i))
                stp.check()
            group(G_E + 3, {}, sigmoids(3))
            act.wait_ge(piece_done, G_F * NP)
            act.wait_ge(mix_ok, KT)
            for k in range(KT):
                act.activation(h_hi[:, k, :], feat[:, k, :], ACT.Copy).then_inc(mix_hi, 1)

            def out_squares(i, stp):
                def f(c):
                    act.wait_ge(free[c], i + (G_F + 1))
                    stp(act.activation(fjunk, y[c][:, bass.ds(i * GW, GW)], ACT.Square,
                                       accum_out=rs[:, bass.ds(i + 4 * c, 1)]))
                return f

            with act.Fori(0, 3) as i:
                stp = Steps(act, a_f, i, 4)
                group(i + G_F, {}, out_squares(i, stp))
            group(G_F + 3, {}, lambda c: None)
            for c in range(NT):
                act.wait_ge(free[c], G_END)
                step(act.activation(fjunk, y[c][:, 3 * GW:], ACT.Square, accum_out=rs[:, 4 * c + 3:4 * c + 4]))
                act.sem_inc(yss, 1)
                act.wait_ge(ysum, c + 1)
                step(act.activation(rsum[:, c:c + 1], rsum[:, c:c + 1], ACT.Sqrt, bias=cst[:, 2:3], scale=1.0 / D))
                act.sem_inc(yrt, 1)

        @block.vector
        def _(dve):
            step = Steps(dve, v_step)

            def split(G, p):
                q = p + LEAD
                if isinstance(G, int) and G * NP + q >= G_END * NP:
                    return
                dve.wait_ge(hi_ok, G * NP + (q + 1))
                dve.tensor_tensor(w_lo[:, q % SPL, :, :], raw[:, q % RAW, :, :], w_hi[:, q % SPL, :, :],
                                  ALU.subtract).then_inc(lo_ok, 1)

            def group(G, tasks, take):
                for p in range(NP):
                    split(G, p)
                    for f in tasks.get(p, ()):
                        f()
                for c in range(4):
                    wait_bank(dve, G, c)
                    take(c)

            def head(H, X, nx, step, slot, slots, q_tile, k_tile, g_tile):
                q, k = feat[:, q_tile, :], feat[:, k_tile, :]

                def halves(ap, s):
                    v = ap.rearrange("p (b two s) -> p b two s", two=2, s=s)
                    return v[:, :, 0, :], v[:, :, 1, :]

                def arg(l):
                    s = LV[l - 1]
                    bk, bq = halves(bcum[:, :], s)
                    ek, eq = halves(ex[EXL[l]][:, :], s)
                    ref = bk[:, :, s - 1:s].to_broadcast([P, T // (2 * s), s])
                    step(dve.tensor_tensor(ek, ref, bk, ALU.subtract))
                    step(dve.tensor_tensor(eq, bq, ref, ALU.subtract))
                    dve.sem_inc(arg_ok, 1)

                def scale(l):
                    s = LV[l - 1]
                    dve.wait_ge(exp_ok, H * NEXP + (4 + l))
                    step(dve.tensor_tensor(kl[l % 2][:, :], k, ex[EXL[l]][:, :], ALU.mult))
                    _, qh = halves(q, s)
                    _, eq = halves(ex[EXL[l]][:, :], s)
                    step(dve.tensor_tensor(ql[l % 2][:, 0:T // 2].rearrange("p (b s) -> p b s", s=s), qh, eq, ALU.mult))
                    dve.sem_inc(lvl_ok, 1)

                def scores(l):
                    dve.wait_ge(sc_ps, H * NL + (l + 1))
                    dve.sem_inc(sc_seen, 1)
                    if l == 0:
                        step(dve.copy_predicated(att[:, :], mask0[:, :], sc[0][:, :]))
                    else:
                        s = LV[l - 1]
                        _, a = halves(att[:, :], s)
                        step(dve.copy_predicated(a, maskl[l - 1][:, :].rearrange("p (b s) -> p b s", s=s),
                                                 sc[l % 2][:, 0:T // 2].rearrange("p (b s) -> p b s", s=s)))
                    dve.sem_inc(sc_ok, 1)

                def first():
                    if nx == 1:
                        dve.wait_ge(g_ok, X - 7)
                    step(dve.tensor_tensor_scan(bcum[:, :], reset[:, :], gdec[:, :] if nx == 1 else feat[:, g_tile, :],
                                                0.0, ALU.mult, ALU.add))
                    dve.sem_inc(arg_ok, 1)
                    bc = bcum[:, :].rearrange("p (c n) -> p c n", c=NT)[:, 0:3, :]
                    step(dve.tensor_tensor(ex[2][:, 0:3 * P].rearrange("p (c n) -> p c n", c=3),
                                           bc[:, :, P - 1:P].to_broadcast([P, 3, P]), bc, ALU.subtract))
                    dve.sem_inc(arg_ok, 1)
                    b4 = bcum[:, :].rearrange("p (b r) -> p b r", r=4)
                    step(dve.tensor_tensor(mid[:, :], b4[:, :, 1], b4[:, :, 2], ALU.add))
                    step(dve.scalar_tensor_tensor(out=ex[0][:, :].rearrange("p (b r) -> p b r", r=4),
                                                  in0=mid[:, :].rearrange("p (b o) -> p b o", o=1).to_broadcast([P, P, 4]),
                                                  scalar=-0.5, in1=b4, op0=ALU.mult, op1=ALU.add))
                    dve.sem_inc(arg_ok, 1)
                    if nx == 1:
                        dve.wait_ge(k_ok, X - 7)
                    dve.wait_ge(exp_ok, H * NEXP + 1)
                    step(dve.tensor_tensor(kd[:, :], k[:, 0:3 * P], ex[2][:, 0:3 * P], ALU.mult))
                    dve.sem_inc(kd_ok, 1)
                    arg(1)
                    dve.wait_ge(exp_ok, H * NEXP + 2)
                    step(dve.tensor_tensor(qe[:, :], q[:, P:T], ex[3][:, 0:3 * P], ALU.mult))
                    step(dve.tensor_copy(dec[:, :], ex[3][:, 0:2 * P].rearrange("p (c n) -> p c n", c=2)[:, :, P - 1]))
                    dve.wait_ge(exp_ok, H * NEXP + 3)
                    step(dve.tensor_tensor(kl[0][:, :], k, ex[1][:, :], ALU.mult))
                    dve.wait_ge(exp_ok, H * NEXP + 4)
                    step(dve.tensor_tensor(ql[0][:, :], q, ex[0][:, :], ALU.mult))
                    dve.sem_inc(lvl_ok, 1)
                    arg(2)

                def second():
                    scale(1)
                    arg(3)
                    scores(0)
                    scale(2)
                    arg(4)

                def third():
                    scores(1)
                    scale(3)
                    arg(5)
                    scores(2)
                    scale(4)
                    states(0)()
                    scores(3)
                    scale(5)

                def states(xx):
                    def f():
                        dve.wait_ge(u_ps, X + (xx + 1))
                        step(dve.tensor_copy(state[:, 0:P], st[:, 0:P]))
                        for c in (1, 2):
                            step(dve.scalar_tensor_tensor(out=state[:, c * P:(c + 1) * P], in0=state[:, (c - 1) * P:c * P],
                                                          scalar=dec[:, c - 1:c], in1=st[:, c * P:(c + 1) * P],
                                                          op0=ALU.mult, op1=ALU.add))
                        dve.sem_inc(s_ok, 1)
                    return f

                def fourth():
                    scores(4)
                    scores(5)

                def norm():
                    dve.wait_ge(rstd_ok, H + 1)
                    for xx in range(nx):
                        o = feat[:, q_tile + xx, :]
                        step(dve.scalar_tensor_tensor(out=o, in0=o, scalar=par[:, bass.ds(X + (R_GNW + xx), 1)],
                                                      in1=sq[:, :], op0=ALU.mult, op1=ALU.mult))

                todo = {}
                for name, f in (("first", first), ("second", second), ("third", third), ("fourth", fourth),
                                ("states1", states(1)), ("norm", norm)):
                    if name in slots:
                        todo.setdefault(slots[name], []).append(f)
                return todo

            for j, v in enumerate((EPS * 2.0 ** -LN_SHIFT, -0.5 * LN_SHIFT * LN2, EPS, 1.0)):
                step(dve.memset(cst[:, j:j + 1], v))
            dve.sem_inc(consts, 1)
            for w in (w_hi, w_lo):
                step(dve.memset(w[:, SPL - 1, :, :].bitcast(F32), 0.0))
            dve.sem_inc(lrw_zero, 1)

            def normalise(t):
                dve.wait_ge(xss, t + 1)
                step(dve.reciprocal(rs[:, t:t + 1], rs[:, t:t + 1]))
                step(dve.scalar_tensor_tensor(out=xin[:, t, :], in0=xin[:, t, :], scalar=rs[:, t:t + 1], in1=nwb,
                                              op0=ALU.mult, op1=ALU.mult))
                dve.sem_inc(xn_ok, 1)

            def lows(t):
                for j in range(4):
                    dve.wait_ge(xt_hi, 4 * t + j + 1)
                    h = (slice(None), slice(4 * j, 4 * j + 4), slice(t * P, (t + 1) * P))
                    dve.tensor_tensor(h_lo[h], main[j][:, :].rearrange("p (a n) -> p a n", a=4), h_hi[h],
                                      ALU.subtract).then_inc(xt_lo, 1)

            dve.wait_ge(nw_in, 16)
            normalise(0)
            normalise(1)
            lows(0)
            normalise(2)
            lows(1)
            normalise(3)
            lows(2)
            dve.wait_ge(lrw_hi, 1)
            for a, w in enumerate((w_hi, w_lo)):
                step(dve.tensor_tensor(lrw(w)[:, :, LOWRANK:2 * LOWRANK], lr_raw[:, 8 * a:8 * a + 8, :],
                                       lrw(w)[:, :, 0:LOWRANK], ALU.subtract))
            dve.sem_inc(lrw_ok, 1)
            for p in range(-LEAD, 0):
                split(0, p)
            lows(3)
            dve.wait_ge(par_ps, 1)
            step(dve.tensor_copy(par[:, :], po[:, 0:R_END]))
            l0, l1 = par[:, 0:HG_H], par[:, HG_H:2 * HG_H]
            step(dve.tensor_tensor(lb[:, :], l0, l1, ALU.max))
            step(dve.tensor_tensor(lbt[:, 0:HG_H], l0, lb[:, :], ALU.subtract))
            step(dve.tensor_tensor(lbt[:, HG_H:2 * HG_H], l1, lb[:, :], ALU.subtract))
            dve.sem_inc(lb_arg, 1)
            dve.wait_ge(lb_e, 1)
            step(dve.tensor_tensor(oml[:, :], lbt[:, 0:HG_H], lbt[:, HG_H:2 * HG_H], ALU.add))
            step(dve.reciprocal(oml[:, :], oml[:, :]))
            step(dve.tensor_tensor(lb[:, :], lbt[:, 0:HG_H], oml[:, :], ALU.mult))
            step(dve.tensor_scalar(oml[:, :], lb[:, :], -1.0, 1.0, ALU.mult, ALU.add))
            step(dve.tensor_scalar(noml[:, :], lb[:, :], 1.0, -1.0, ALU.mult, ALU.add))
            step(dve.tensor_scalar(lb[:, :], lb[:, :], LB_MIN, None, ALU.max))
            dve.sem_inc(lb_ok, 1)
            dve.wait_ge(consts, 3)

            def decays():
                for h, bank in enumerate((sc[0], sc[1], po, st)):
                    dve.wait_ge(z_abs, h + 1)
                    step(dve.tensor_scalar(gdec[:, :], bank[:, :], par[:, R_BUP + h:R_BUP + h + 1], 0.0, ALU.add, ALU.min))
                    g = feat[:, T_GA + h, :]
                    step(dve.tensor_tensor(g, gdec[:, :], ex[2 + h % 2][:, :], ALU.subtract))
                    dve.sem_inc(z_ok, 1)
                    step(dve.tensor_scalar(g, g, 1.0 / TAU, G_MIN, ALU.mult, ALU.max))

            def values(half):
                def f(c):
                    dve.tensor_copy(val[:, c, bass.ds(half * GW, GW)], main[c][:, :]).then_inc(free[c], 1)
                return f

            group(0, {1: [decays]}, lambda c: None)
            group(1, {}, lambda c: None)
            with dve.Fori(0, 2) as i:
                group(i + G_V, {}, values(i))
            gla = dict(first=0, second=1, third=2, fourth=3, states1=5, norm=6)
            with dve.Fori(0, 2) as i:
                stp = Steps(dve, v_c, i, V_C)
                for a in range(2):
                    H = i * 2 + a
                    group(i * 2 + (G_C + a), head(H, H * 2, 2, stp, 0, gla, H * 2, H * 2 + 1, H + T_GA), lambda c: None)
                stp.check()

            def hg_pair(m, stp):
                todo = {}
                for u in range(2):
                    z = 4 * u
                    for q, fs in head(m + (GLA_H + u), m + (8 + u), 1, stp, u,
                                      dict(first=z, second=z + 1, third=z + 2, fourth=z + 3, norm=z + 3),
                                      m + (T_HQ + u), m + (T_HF + u), None).items():
                        todo.setdefault(q, []).extend(fs)
                return todo

            def gates(e, stp):
                def f(c):
                    dve.wait_ge(gate_ok, e * 4 + (c + 1))
                    stp(dve.tensor_tensor(gate[:, :], main[c][:, :], gate[:, :], ALU.mult))
                    dve.sem_inc(free[c], 1)
                    o = feat[:, e * 4 + c, :]
                    stp(dve.tensor_tensor(o, o, gate[:, :], ALU.mult))
                    dve.sem_inc(gate_used, 1)
                return f

            group(G_D, {}, values(0))
            group(G_D + 1, hg_pair(0, step), values(1))
            with dve.Fori(0, 3) as i:
                stp = Steps(dve, v_e, i, V_E)
                group(i + G_E, hg_pair(i * 2 + 2, stp), gates(i, stp))
                stp.check()
            group(G_E + 3, {}, gates(3, step))
            dve.sem_inc(mix_ok, KT)
            for k in range(KT):
                dve.wait_ge(mix_hi, k + 1)
                dve.tensor_tensor(h_lo[:, k, :], feat[:, k, :], h_hi[:, k, :], ALU.subtract).then_inc(mix_lo, 1)
            def residual(i):
                def f(c):
                    dve.wait_ge(x2_in, 16 * NT)
                    o = y[c][:, bass.ds(i * GW, GW)]
                    dve.tensor_tensor(o, o, main[c][:, :], ALU.add).then_inc(free[c], 1)
                return f

            with dve.Fori(0, 3) as i:
                group(i + G_F, {}, residual(i))
            group(G_F + 3, {}, residual(3))
            dve.wait_ge(fn_in, 16)
            for c in range(NT):
                dve.wait_ge(yss, c + 1)
                step(dve.tensor_reduce(rsum[:, c:c + 1], rs[:, 4 * c:4 * c + 4], mybir.AxisListType.X, ALU.add))
                dve.sem_inc(ysum, 1)
                dve.wait_ge(yrt, c + 1)
                step(dve.reciprocal(rsum[:, c:c + 1], rsum[:, c:c + 1]))
                dve.scalar_tensor_tensor(out=y[c], in0=y[c], scalar=rsum[:, c:c + 1], in1=fnb,
                                         op0=ALU.mult, op1=ALU.mult).then_inc(yn, 1)


def kernel(x, norm_w, w_in, gla_w_up, gla_b_up, gla_norm_w, hgrn_lb_logits, hgrn_norm_w, w_out, final_norm_w):
    import numpy as np
    import concourse.bacc as bacc
    from concourse.bass_utils import run_bass_kernel_spmd

    given = {
        "x": np.asarray(x).reshape(T, D), "norm_w": np.asarray(norm_w).reshape(D),
        "w_in": np.asarray(w_in)[0], "gla_w_up": np.asarray(gla_w_up)[0],
        "gla_b_up": np.asarray(gla_b_up).reshape(GLA_H, P), "gla_norm_w": np.asarray(gla_norm_w).reshape(8, P),
        "lb_logits": np.asarray(hgrn_lb_logits).reshape(2 * HG_H, P),
        "hgrn_norm_w": np.asarray(hgrn_norm_w).reshape(HG_H, P), "w_out": np.asarray(w_out)[0],
        "final_norm_w": np.asarray(final_norm_w),
    }
    nc = bacc.Bacc("TRN2", target_bir_lowering=False, num_devices=1)
    arrays, args = {}, {}
    for name, a in given.items():
        a = np.ascontiguousarray(a)
        arrays[f"in_{name}"] = a
        args[name] = nc.dram_tensor(f"in_{name}", a.shape, mybir.dt.from_np(a.dtype), kind="ExternalInput").ap()
    args["out"] = nc.dram_tensor("out_y", (T, D), F32, kind="ExternalOutput").ap()
    hymba_kernel(nc, **args)
    r = run_bass_kernel_spmd(nc, [arrays], core_ids=[0])
    return r.results[0]["out_y"].reshape(1, T, D)
```

```python
from contextlib import ExitStack

import concourse.bass as bass
from concourse import mybir

ALU = mybir.AluOpType
ACT = mybir.ActivationFunctionType
F32 = mybir.dt.float32
F32R = mybir.dt.float32r
U8 = mybir.dt.uint8

P = 128
T = 512
D = 2048
NT = T // P
KT = D // P
GLA_H, HG_H = 4, 8
LOWRANK = 16
TAU = 16.0
EPS = 1e-6
SCALE = float(P) ** -0.5
GW = 512
PK = 2
NP = KT // PK
RAW, SPL = 2, 4
LEAD = 3

C_GQ, C_GK, C_GV, C_GG = 0, 512, 1024, 2048
C_LR = 3072
C_HQ, C_HF, C_HI, C_HG = 3088, 4112, 5136, 6160
G_V, G_A, G_C, G_D, G_E, G_F, G_END = 0, 2, 4, 8, 10, 14, 18
HP = NP // 2
LNEXP = "natural_log_exp_and_others"

LV = [4, 8, 16, 32, 64]
NL = 1 + len(LV)
NEXP = 3 + len(LV) + 1
NARG = 3 + len(LV)
R_LOG, R_BUP, R_GNW, R_HNW, R_END = 0, 16, 20, 28, 36
T_HQ, T_HF, T_GA = 8, 16, 20
LN_SHIFT = 2
G_MIN = -50.0
LB_MIN = 2.0 ** -60


EXL = [None, 2, 3, 0, 1, 3]
LN2 = 0.6931471805599453
A_C, A_E, V_C, V_E = 26, 28, 86, 78


class Steps:

    def __init__(self, eng, sem, i=0, per=0):
        self.eng, self.sem, self.i, self.per, self.n = eng, sem, i, per, 0

    def __call__(self, ins):
        self.n += 1
        ins.then_inc(self.sem, 1)
        self.eng.wait_ge(self.sem, self.i * self.per + self.n)
        return ins

    def check(self):
        assert self.n == self.per, (self.sem, self.n)


def hymba_kernel(nc, x, norm_w, w_in, gla_w_up, gla_b_up, gla_norm_w, lb_logits, hgrn_norm_w, w_out,
                 final_norm_w, out):
    with ExitStack() as ctx:
        def sb(name, shape, dt=F32):
            return ctx.enter_context(nc.sbuf_tensor(name, shape, dt))

        def ps(name):
            return ctx.enter_context(nc.psum_tensor(name, [P, 512], F32))

        def sem(name):
            return ctx.enter_context(nc.semaphore(name))

        h_hi = sb("h_hi", [P, KT, T], F32R)
        h_lo = sb("h_lo", [P, KT, T], F32R)
        raw = sb("raw", [P, RAW, PK, GW])
        w_hi = sb("w_hi", [P, SPL, PK, GW], F32R)
        w_lo = sb("w_lo", [P, SPL, PK, GW], F32R)
        feat = sb("feat", [P, 24, T])
        val = sb("val", [P, NT, 1024])
        reset = sb("reset", [P, T], U8)
        bcum = sb("bcum", [P, T])
        gdec = sb("gdec", [P, T])
        ex = [sb(f"ex{i}", [P, T]) for i in range(4)]
        kl = [sb(f"kl{i}", [P, T]) for i in range(2)]
        ql = [sb("ql0", [P, T]), sb("ql1", [P, T // 2])]
        kd = sb("kd", [P, 3 * P])
        kdT = sb("kdT", [P, 3 * P])
        qe = [sb(f"qe{i}", [P, 3 * P]) for i in range(2)]
        att = sb("att", [P, T])
        state = sb("state", [P, 3 * P])
        vst = [sb(f"vst{i}", [P, NT, P]) for i in range(2)]
        sq = sb("sq", [P, T])
        mask0 = sb("mask0", [P, P], U8)
        lrw = sb("lrw", [P, KT, 2 * LOWRANK], F32R)
        maskl = [sb(f"mask{s}", [P, T // 2], U8) for s in LV]
        ones = sb("ones", [P, P])
        ident = sb("ident", [P, P])
        par = sb("par", [P, R_END])
        lb = sb("lb", [P, HG_H])
        oml = sb("oml", [P, HG_H])
        noml = sb("noml", [P, HG_H])
        cst = sb("cst", [P, 4])
        lbt = sb("lbt", [P, 2 * HG_H])
        dec = sb("dec", [P, 2])
        rsum = sb("rsum", [P, NT])
        rs = sb("rs", [P, 4 * NT])

        main = [ps(f"main{c}") for c in range(4)]
        sc = [ps("sc0"), ps("sc1")]
        po = ps("po")
        st = ps("st")
        side = [sc[0], sc[1], po, st]

        xin = feat[:, 0:16, :].rearrange("p (t a) n -> p t (a n)", t=NT)
        nwb = feat[:, 16:20, :].rearrange("p a n -> p (a n)")
        nrow = val[0:1, 0:2, :].rearrange("p a n -> p (a n)")
        mid = kd[:, 0:P]
        junk = feat[:, 20:24, :].rearrange("p a n -> p (a n)")
        lr_raw = bcum[:, 0:KT * LOWRANK].rearrange("p (k r) -> p k r", k=KT)
        lr = ex[0]
        wup = ex[1]
        prow = ex[3]
        y = [val[:, 0:2, :].rearrange("p a n -> p (a n)"), val[:, 2:4, :].rearrange("p a n -> p (a n)"),
             feat[:, 16:20, :].rearrange("p a n -> p (a n)"), feat[:, 20:24, :].rearrange("p a n -> p (a n)")]
        fnb = feat[:, 0:4, :].rearrange("p a n -> p (a n)")
        fjunk = feat[:, 4:5, :].rearrange("p a n -> p (a n)")

        x_in = [sem(f"x_in{t}") for t in range(NT)]
        nw_in = sem("nw_in")
        par_in = sem("par_in")
        lr_in = sem("lr_in")
        up_in = sem("up_in")
        raw_in = [sem(f"raw_in{s}") for s in range(RAW)]
        x2_in = sem("x2_in")
        fn_in = sem("fn_in")
        out_done = sem("out_done")
        consts = sem("consts")
        cst_ok = sem("cst_ok")
        a_step, v_step, p_step = sem("a_step"), sem("v_step"), sem("p_step")
        a_c, v_c = sem("a_c"), sem("v_c")
        a_e, v_e = sem("a_e"), sem("v_e")
        y_act, lb_arg, lb_ok, z_ok, k_ok, gate_used, y_fn, ysum, yrt = (sem(n) for n in (
            "y_act", "lb_arg", "lb_ok", "z_ok", "k_ok", "gate_used", "y_fn", "ysum", "yrt"))
        sc_seen = sem("sc_seen")
        xss = sem("xss")
        xn_ok = sem("xn_ok")
        xt_ps, xt_hi, xt_lo = sem("xt_ps"), sem("xt_hi"), sem("xt_lo")
        par_ps, par_ok = sem("par_ps"), sem("par_ok")
        lb_e = sem("lb_e")
        lrw_hi, lrw_ok, lr_ps, lr_ok, z_ps, z_abs = (sem(n) for n in ("lrw_hi", "lrw_ok", "lr_ps", "lr_ok", "z_ps", "z_abs"))
        hi_ok, lo_ok, piece_done = sem("hi_ok"), sem("lo_ok"), sem("piece_done")
        full = sem("full")
        free = [sem(f"free{c}") for c in range(4)]
        g_ok = sem("g_ok")
        gate_ok = sem("gate_ok")
        nb_ps, nb_ok, y_sq = sem("nb_ps"), sem("nb_ok"), sem("y_sq")
        arg_ok, exp_ok, kd_ok = sem("arg_ok"), sem("exp_ok"), sem("kd_ok")
        kT_ps, kT_ok, v_ok = sem("kT_ps"), sem("kT_ok"), sem("v_ok")
        lvl_ok, sc_ps, sc_ok = sem("lvl_ok"), sem("sc_ps"), sem("sc_ok")
        u_ps, s_ok, o_ps, sq_ok, ms_ps, rstd_ok = (sem(n) for n in ("u_ps", "s_ok", "o_ps", "sq_ok", "ms_ps", "rstd_ok"))
        mix_hi, mix_lo = sem("mix_hi"), sem("mix_lo")
        yss, yn = sem("yss"), sem("yn")

        def wait_bank(eng, G, c):
            if c < 3:
                eng.wait_ge(full, G * 3 + (c + 1))
            else:
                eng.wait_ge(piece_done, G * NP + NP)

        block = ctx.enter_context(nc.Block())

        @block.sync
        def _(sp):
            def group(src, col, G, pieces=range(NP)):
                for p in pieces:
                    n = NP * G + p
                    s = p % RAW
                    if not (isinstance(n, int) and n < RAW):
                        sp.wait_ge(lo_ok, n - RAW + 1)
                    rows = src[p * PK * P:(p + 1) * PK * P, bass.ds(col, GW)]
                    sp.dma_start(raw[:, s, :, :], rows.rearrange("(k p) n -> p k n", p=P)).then_inc(raw_in[s], 16)

            sp.dma_start(nrow, norm_w.rearrange("(o n) -> o n", o=1)).then_inc(nw_in, 16)
            group(w_in, C_GV, G_V)
            group(w_in, C_GV + GW, G_V + 1)
            with sp.Fori(0, 2) as i:
                group(w_in, i * GW + C_GQ, i + G_A)
            with sp.Fori(0, 2) as i:
                group(w_in, i * GW + C_HQ, i * 2 + G_C)
                group(w_in, i * GW + C_HF, i * 2 + (G_C + 1))
            with sp.Fori(0, 2) as i:
                group(w_in, i * GW + C_HI, i + G_D)
            with sp.Fori(0, 2) as i:
                group(w_in, i * GW + C_GG, i + G_E)
            with sp.Fori(0, 2) as i:
                group(w_in, i * GW + C_HG, i + (G_E + 2))
            group(w_out, 0, G_F, range(LEAD + 1))
            sp.wait_ge(mix_lo, KT)
            for t in range(NT):
                sp.dma_start(y[t], x[t * P:(t + 1) * P, :]).then_inc(x2_in, 16)
            sp.dma_start(fnb, final_norm_w.partition_broadcast(P)).then_inc(fn_in, 16)
            group(w_out, 0, G_F, range(LEAD + 1, NP))
            with sp.Fori(0, 3) as i:
                group(w_out, i * GW + GW, i + (G_F + 1))
            for t in range(NT):
                sp.wait_ge(yn, t + 1)
                sp.dma_start(out[t * P:(t + 1) * P, D // 2:], y[t][:, D // 2:]).then_inc(out_done, 16)
            sp.wait_ge(out_done, 2 * 16 * NT)

        @block.gpsimd
        def _(pool):
            n = [0]

            def step(ins):
                n[0] += 1
                ins.then_inc(p_step, 1)
                pool.wait_ge(p_step, n[0])

            step(pool.memset(ones[:, :], 1.0))
            step(pool.memset(ident[:, :], 0.0))
            step(pool.affine_select(out=ident[:, :], in_=ident[:, :], compare_op=ALU.not_equal, fill=1.0, base=0,
                                    pattern=[[-1, P]], channel_multiplier=1))
            pool.sem_inc(consts, 1)
            step(pool.memset(reset[:, :], 1.0))
            step(pool.memset(reset[:, :].rearrange("p (c n) -> p c n", c=NT)[:, :, 0:1], 0.0))
            m = gdec[:, 0:P]
            step(pool.memset(m[:, :], 1.0))
            step(pool.affine_select(out=m[:, :], in_=m[:, :], compare_op=ALU.is_ge, fill=0.0, base=0,
                                    pattern=[[-4, P // 4], [0, 4]], channel_multiplier=1))
            step(pool.affine_select(out=m[:, :], in_=m[:, :], compare_op=ALU.is_ge, fill=0.0, base=0,
                                    pattern=[[4, P // 4], [1, 4]], channel_multiplier=-1))
            step(pool.tensor_copy(mask0[:, :], m[:, :]))
            for s, mk in zip(LV, maskl):
                m = gdec[:, 0:T // 2]
                step(pool.memset(m, 1.0))
                step(pool.affine_select(out=m, in_=m, compare_op=ALU.is_ge, fill=0.0, base=0,
                                        pattern=[[0, NT], [-2 * s, P // (2 * s)], [0, s]], channel_multiplier=1))
                step(pool.affine_select(out=m, in_=m, compare_op=ALU.is_ge, fill=0.0, base=s - 1,
                                        pattern=[[0, NT], [2 * s, P // (2 * s)], [0, s]], channel_multiplier=-1))
                step(pool.tensor_copy(mk[:, :], m))
            step(pool.memset(att[:, :], 0.0))
            pool.sem_inc(consts, 1)

        @block.tensor
        def _(pe):
            def products(p, c, tokens_stationary):
                s = p % SPL
                cs = slice(c * P, (c + 1) * P)
                for kk in range(PK):
                    k = p * PK + kk
                    if tokens_stationary:
                        pairs = [(h_hi[:, k, cs], w_hi[:, s, kk, :]), (h_hi[:, k, cs], w_lo[:, s, kk, :]),
                                 (h_lo[:, k, cs], w_hi[:, s, kk, :])]
                    else:
                        pairs = [(w_hi[:, s, kk, cs], h_hi[:, k, :]), (w_hi[:, s, kk, cs], h_lo[:, k, :]),
                                 (w_lo[:, s, kk, cs], h_hi[:, k, :])]
                    for j, (a, b) in enumerate(pairs):
                        mm = pe.matmul(main[c][:, :], a, b, start=(k == 0 and j == 0), stop=(k == KT - 1 and j == 2))
                if c == 3:
                    mm.then_inc(piece_done, 1)
                elif p == NP - 1:
                    mm.then_inc(full, 1)

            def group(G, tokens_stationary, tasks=None, pieces=range(NP), before=lambda p: None):
                tasks = tasks or {}
                for p in pieces:
                    before(p)
                    pe.wait_ge(lo_ok, G * NP + (p + 1))
                    for c in range(4):
                        if p == 0:
                            pe.wait_ge(free[c], G * 1)
                        products(p, c, tokens_stationary)
                        for f in tasks.get(4 * p + c, ()):
                            f()

            def by_tile(G, pieces, between=lambda p, c: None):
                for c in range(4):
                    for p in pieces:
                        if c == 0:
                            pe.wait_ge(lo_ok, G * NP + (p + 1))
                        products(p, c, True)
                        between(p, c)

            def head_tasks(H, X, nx, at):
                def transposes():
                    pe.wait_ge(kd_ok, H + 1)
                    for c in range(3):
                        mm = pe.transpose(st[:, c * P:(c + 1) * P], kd[:, c * P:(c + 1) * P], ident[:, :])
                    mm.then_inc(kT_ps, 1)

                def level(l):
                    def f():
                        pe.wait_ge(lvl_ok, H * NL + (l + 1))
                        if l >= 2:
                            pe.wait_ge(sc_ok, H * NL + (l - 1))
                        elif l == 0 and nx == 1:
                            pe.wait_ge(rstd_ok, H * 1)
                        w = P if l == 0 else P // 2
                        for c in range(NT):
                            mm = pe.matmul(sc[l % 2][:, c * w:(c + 1) * w], kl[l % 2][:, c * P:(c + 1) * P],
                                           ql[l % 2][:, c * w:(c + 1) * w], start=True, stop=True)
                        mm.then_inc(sc_ps, 1)
                    return f

                def update(xx):
                    def f():
                        if xx == 0:
                            pe.wait_ge(kT_ok, H + 1)
                        pe.wait_ge(v_ok, X + (xx + 1))
                        for c in range(3):
                            mm = pe.matmul(st[:, c * P:(c + 1) * P], kdT[:, c * P:(c + 1) * P], vst[vs(xx)][:, c, :],
                                           start=True, stop=True)
                        mm.then_inc(u_ps, 1)
                    return f

                def outputs(xx):
                    def f():
                        pe.wait_ge(sc_ok, H * NL + NL)
                        pe.wait_ge(s_ok, X + (xx + 1))
                        for c in range(NT):
                            cs = slice(c * P, (c + 1) * P)
                            mm = pe.matmul(po[:, cs], vst[vs(xx)][:, c, :], att[:, cs], start=True, stop=(c == 0))
                            if c:
                                mm = pe.matmul(po[:, cs], state[:, (c - 1) * P:c * P], qe[at["slot"]][:, (c - 1) * P:c * P],
                                               start=False, stop=True)
                        mm.then_inc(o_ps, 1)
                    return f

                def meansq(xx):
                    def f():
                        pe.wait_ge(sq_ok, X + (xx + 1))
                        mm = pe.matmul(sc[0][:, :], ones[:, :], sq[:, :], start=(xx == 0), stop=(xx == nx - 1))
                        if xx == nx - 1:
                            mm.then_inc(ms_ps, 1)
                    return f

                def vs(xx):
                    return xx if nx == 2 else at["slot"]

                todo = {}
                todo.setdefault(at["T"], []).append(transposes)
                for l in range(NL):
                    todo.setdefault(at["L"][l], []).append(level(l))
                for xx in range(nx):
                    todo.setdefault(at["U"][xx], []).append(update(xx))
                    todo.setdefault(at["O"][xx], []).append(outputs(xx))
                    todo.setdefault(at["M"][xx], []).append(meansq(xx))
                return todo

            pe.wait_ge(consts, 1)
            pe.wait_ge(nw_in, 16)
            for j in range(4):
                pe.matmul(main[j][:, :], ones[0:1, :], nrow[:, j * 512:(j + 1) * 512], start=True,
                          stop=True).then_inc(nb_ps, 1)

            def transposes(t):
                pe.wait_ge(xn_ok, t + 1)
                for j in range(4):
                    if t:
                        pe.wait_ge(xt_lo, 4 * (t - 1) + j + 1)
                    for k in range(4 * j, 4 * j + 4):
                        mm = pe.transpose(side[j][:, (k % 4) * P:(k % 4 + 1) * P], xin[:, t, k * P:(k + 1) * P], ident[:, :])
                    mm.then_inc(xt_ps, 1)

            def between(p, c):
                if p == 1 and c < 3:
                    transposes(c + 1)
                if p == HP - 1 and c < 3:
                    pe.wait_ge(xt_lo, 4 * (c + 2))

            def low_rank():
                pe.wait_ge(lrw_ok, 1)
                for k in range(KT):
                    pe.matmul(st[0:2 * LOWRANK, :], lrw[:, k, :], h_hi[:, k, :], start=(k == 0), stop=False)
                    mm = pe.matmul(st[0:2 * LOWRANK, :], lrw[:, k, :], h_lo[:, k, :], start=False, stop=(k == KT - 1))
                mm.then_inc(lr_ps, 1)

            def parameters():
                pe.wait_ge(par_in, 64)
                pe.transpose(po[:, 0:R_END], prow[0:R_END, 0:P], ident[0:R_END, 0:R_END]).then_inc(par_ps, 1)

            def decay_inputs():
                pe.wait_ge(lr_ok, 1)
                pe.wait_ge(up_in, 32)
                for h, bank in enumerate(side):
                    mm = pe.matmul(bank[:, :], wup[0:2 * LOWRANK, h * P:(h + 1) * P], lr[0:2 * LOWRANK, :],
                                   start=True, stop=True)
                    mm.then_inc(z_ps, 1)

            pe.wait_ge(nb_ok, 4)
            transposes(0)
            pe.wait_ge(xt_lo, 4)
            by_tile(0, range(HP), between)
            group(0, True, {31: [parameters]}, range(HP, NP))
            group(1, True, {8: [low_rank], 16: [decay_inputs]})
            with pe.Fori(0, 2) as i:
                group(i + G_A, False)
            gla_at = dict(slot=0, T=7, L=[9, 11, 12, 14, 15, 17], U=[13, 22], O=[19, 24], M=[21, 26])
            with pe.Fori(0, 2) as i:
                for a in range(2):
                    H = i * 2 + a
                    group(i * 2 + (G_C + a), False, head_tasks(H, H * 2, 2, gla_at))

            def hg_at(u):
                z = 16 * u
                return dict(slot=u, T=z, L=[z + q for q in (1, 2, 4, 6, 8, 9)], U=[z + 3], O=[z + 10], M=[z + 12])

            def hg_pair(m):
                return head_tasks(m + GLA_H, m + 8, 1, hg_at(0)) | head_tasks(m + (GLA_H + 1), m + 9, 1, hg_at(1))

            group(G_D, True)
            group(G_D + 1, True, hg_pair(0))
            with pe.Fori(0, 2) as i:
                group(i + G_E, False, hg_pair(i * 2 + 2))
            group(G_E + 2, False, hg_pair(6))
            group(G_E + 3, False)
            group(G_F, True, before=lambda p: pe.wait_ge(mix_lo, PK * (p + 1)))
            with pe.Fori(0, 2) as i:
                group(i + (G_F + 1), True)
            group(G_F + 3, True, pieces=range(HP))
            by_tile(G_F + 3, range(HP, NP))

        @block.scalar
        def _(act):
            step = Steps(act, a_step)

            def split(G, p):
                q = p + LEAD
                if isinstance(G, int) and G * NP + q >= G_END * NP:
                    return
                act.wait_ge(raw_in[q % RAW], G * (NP // RAW * 16) + 16 * (q // RAW + 1))
                if not (isinstance(G, int) and G * NP + q < SPL):
                    act.wait_ge(piece_done, G * NP + (q - SPL + 1))
                act.activation(w_hi[:, q % SPL, :, :], raw[:, q % RAW, :, :], ACT.Copy).then_inc(hi_ok, 1)

            def group(G, tasks, take, first=0):
                for p in range(NP):
                    if p >= first:
                        split(G, p)
                    for f in tasks.get(p, ()):
                        f()
                for c in range(4):
                    wait_bank(act, G, c)
                    take(c)

            def head(H, X, nx, step, slot, slots, q_tile):
                def e(n_arg, dst, src, scale=1.0):
                    act.wait_ge(arg_ok, H * NARG + n_arg)
                    step(act.activation(dst, src, ACT.Exp, scale=scale))
                    act.sem_inc(exp_ok, 1)

                def decay():
                    m = X - 8
                    r = feat[:, m + T_HF, :]
                    step(act.activation(gdec[:, :], r, ACT.Ln, bias=lb[:, bass.ds(m, 1)], scale=oml[:, bass.ds(m, 1)]))
                    act.sem_inc(g_ok, 1)
                    step(act.activation(r, r, ACT.Identity, bias=oml[:, bass.ds(m, 1)], scale=noml[:, bass.ds(m, 1)]))
                    act.sem_inc(k_ok, 1)

                def early():
                    e(2, ex[2][:, 0:3 * P], ex[2][:, 0:3 * P])
                    e(2, ex[3][:, 0:3 * P], bcum[:, P:T])
                    e(3, ex[1][:, :], ex[0][:, :], -1.0)
                    e(3, ex[0][:, :], ex[0][:, :])

                def values():
                    for xx in range(nx):
                        col = (X + xx) * P if nx == 2 else (X - 8) * P
                        act.activation(vst[xx if nx == 2 else slot][:, :, :], val[:, :, bass.ds(col, P)],
                                       ACT.Copy).then_inc(v_ok, 1)

                def level(l):
                    def f():
                        e(3 + l, ex[EXL[l]][:, :], ex[EXL[l]][:, :])
                    return f

                def keys():
                    act.wait_ge(kT_ps, H + 1)
                    act.activation(kdT[:, :], st[:, 0:3 * P], ACT.Copy).then_inc(kT_ok, 1)

                def take(xx):
                    def f():
                        act.wait_ge(o_ps, X + (xx + 1))
                        act.activation(feat[:, q_tile + xx, :], po[:, :], ACT.Copy)
                        step(act.activation(sq[:, :], po[:, :], ACT.Square))
                        act.sem_inc(sq_ok, 1)
                    return f

                def rstd():
                    act.wait_ge(ms_ps, H + 1)
                    step(act.activation(sq[:, :], sc[0][:, :], ACT.Ln, bias=cst[:, 0:1],
                                        scale=2.0 ** -LN_SHIFT / (P * nx)))
                    step(act.activation(sq[:, :], sq[:, :], ACT.Exp, bias=cst[:, 1:2], scale=-0.5))
                    act.sem_inc(rstd_ok, 1)

                return dict(decay=decay, early=early, values=values, level=level, keys=keys, take=take, rstd=rstd)

            for t in range(NT):
                act.dma_start(xin[:, t, :], x[t * P:(t + 1) * P, :]).then_inc(x_in[t], 16)
            act.dma_start(prow[R_LOG:R_BUP, 0:P], lb_logits).then_inc(par_in, 16)
            act.dma_start(prow[R_BUP:R_GNW, 0:P], gla_b_up).then_inc(par_in, 16)
            act.dma_start(prow[R_GNW:R_HNW, 0:P], gla_norm_w).then_inc(par_in, 16)
            act.dma_start(prow[R_HNW:R_END, 0:P], hgrn_norm_w).then_inc(par_in, 16)
            act.dma_start(lr_raw, w_in[:, C_LR:C_LR + LOWRANK].rearrange("(k p) r -> p k r", p=P)).then_inc(lr_in, 16)
            for a in range(2):
                act.dma_start(wup[a * LOWRANK:(a + 1) * LOWRANK, :], gla_w_up).then_inc(up_in, 16)
            for j in range(4):
                act.wait_ge(nb_ps, j + 1)
                act.activation(nwb[:, j * 512:(j + 1) * 512], main[j][:, :], ACT.Copy).then_inc(nb_ok, 1)

            act.wait_ge(cst_ok, 1)

            def squares(t):
                act.wait_ge(x_in[t], 16)
                step(act.activation(junk, xin[:, t, :], ACT.Square, accum_out=rs[:, t:t + 1]))
                step(act.activation(rs[:, t:t + 1], rs[:, t:t + 1], ACT.Sqrt, bias=cst[:, 2:3], scale=1.0 / D))
                act.sem_inc(xss, 1)

            def highs(t):
                for j in range(4):
                    act.wait_ge(xt_ps, 4 * t + j + 1)
                    act.activation(h_hi[:, 4 * j:4 * j + 4, t * P:(t + 1) * P],
                                   side[j][:, :].rearrange("p (a n) -> p a n", a=4), ACT.Copy).then_inc(xt_hi, 1)

            squares(0)
            split(0, -3)
            split(0, -2)
            highs(0)
            squares(1)
            split(0, -1)
            split(0, 0)
            highs(1)
            squares(2)
            highs(2)
            squares(3)
            highs(3)
            act.wait_ge(lr_in, 16)
            step(act.activation(lrw[:, :, 0:LOWRANK], lr_raw, ACT.Copy))
            act.sem_inc(lrw_hi, 1)
            act.preload_act_table_set(LNEXP)
            def bounds():
                act.wait_ge(lb_arg, 1)
                step(act.activation(lbt[:, :], lbt[:, :], ACT.Exp))
                act.sem_inc(lb_e, 1)

            def low_rank():
                act.wait_ge(lr_ps, 1)
                act.activation(lr[0:2 * LOWRANK, :], st[0:2 * LOWRANK, :], ACT.Copy).then_inc(lr_ok, 1)

            def decays():
                for h, bank in enumerate(side):
                    act.wait_ge(z_ps, h + 1)
                    if h >= 2:
                        act.wait_ge(z_ok, h - 1)
                    t = ex[2 + h % 2][:, :]
                    step(act.activation(t, bank[:, :], ACT.Abs, bias=par[:, R_BUP + h:R_BUP + h + 1]))
                    step(act.activation(t, t, ACT.Exp, scale=-1.0))
                    step(act.activation(t, t, ACT.Ln, bias=cst[:, 3:4]))
                    act.sem_inc(z_abs, 1)

            def store(tile, scale=1.0, func=ACT.Copy):
                def f(c):
                    act.activation(feat[:, tile(c), :], main[c][:, :], func, scale=scale).then_inc(free[c], 1)
                return f

            group(0, {}, lambda c: None, 1)
            group(1, {0: [bounds], 3: [low_rank], 5: [decays]}, lambda c: None)
            group(G_A, {}, store(lambda c: 2 * c, SCALE))
            group(G_A + 1, {}, store(lambda c: 2 * c + 1))

            def gla_steps(H, stp):
                h = head(H, H * 2, 2, stp, 0, None, H * 2)
                lv = h["level"]
                return {0: [h["early"], h["values"]], 1: [lv(1), h["keys"], lv(2)], 2: [lv(3), lv(4), lv(5)],
                        4: [h["take"](0)], 5: [h["take"](1)], 6: [h["rstd"]]}

            with act.Fori(0, 2) as i:
                stp = Steps(act, a_c, i, A_C)
                group(i * 2 + G_C, gla_steps(i * 2, stp), store(lambda c: i * 4 + (T_HQ + c), SCALE))
                group(i * 2 + (G_C + 1), gla_steps(i * 2 + 1, stp),
                      store(lambda c: i * 4 + (T_HF + c), 1.0, ACT.Sigmoid))
                act.preload_act_table_set(LNEXP)
                stp.check()

            def hg_head(m, u, stp):
                return head(m + (GLA_H + u), m + (8 + u), 1, stp, u % 2, None, m + (8 + u))

            def hg_pair(m, stp, more=True):
                hs = [hg_head(m, u, stp) for u in range(3 if more else 2)]
                todo = {}
                for u in range(2):
                    h, nxt, lv, z = hs[u], hs[u + 1:u + 2], hs[u]["level"], 4 * u
                    todo[z] = [lv(1), h["values"], h["keys"], lv(2)]
                    todo[z + 1] = [lv(3), lv(4)]
                    todo[z + 2] = [lv(5)] + [x["decay"] for x in nxt] + [h["take"](0)]
                    todo[z + 3] = [x["early"] for x in nxt] + [h["rstd"]]
                return todo

            def silu(c):
                act.activation(main[c][:, :], main[c][:, :], ACT.Silu).then_inc(gate_ok, 1)

            h0 = hg_head(0, 0, step)
            group(G_D, {4: [h0["decay"], h0["early"]]}, lambda c: None)
            for c in range(4):
                act.wait_ge(free[c], G_D + 1)
            group(G_D + 1, hg_pair(0, step), lambda c: None)
            for c in range(4):
                act.wait_ge(free[c], G_D + 2)
            with act.Fori(0, 2) as i:
                stp = Steps(act, a_e, i, A_E)
                group(i + G_E, hg_pair(i * 2 + 2, stp), silu)
                act.preload_act_table_set(LNEXP)
                stp.check()
            group(G_E + 2, hg_pair(6, step, False), silu)
            group(G_E + 3, {}, silu)
            for k in range(KT):
                act.wait_ge(free[k % 4], G_E + k // 4 + 1)
                act.activation(h_hi[:, k, :], feat[:, k, :], ACT.Copy).then_inc(mix_hi, 1)

            def out_squares(i, stp):
                def f(c):
                    act.wait_ge(free[c], i + (G_F + 1))
                    stp(act.activation(fjunk, y[c][:, bass.ds(i * GW, GW)], ACT.Square,
                                       accum_out=rs[:, bass.ds(i + 4 * c, 1)]))
                return f

            with act.Fori(0, 3) as i:
                stp = Steps(act, y_sq, i, 4)
                group(i + G_F, {}, out_squares(i, stp))
            for p in range(NP):
                split(G_F + 3, p)
            for c in range(NT):
                act.wait_ge(free[c], G_END)
                step(act.activation(fjunk, y[c][:, 3 * GW:], ACT.Square, accum_out=rs[:, 4 * c + 3:4 * c + 4]))
                act.sem_inc(yss, 1)
                act.wait_ge(ysum, c + 1)
                step(act.activation(rsum[:, c:c + 1], rsum[:, c:c + 1], ACT.Sqrt, bias=cst[:, 2:3], scale=1.0 / D))
                act.sem_inc(yrt, 1)
                act.wait_ge(y_fn, c + 1)
                step(act.activation(y[c][:, 0:D // 2], y[c][:, 0:D // 2], ACT.Copy, scale=rsum[:, c:c + 1]))
                act.dma_start(out[c * P:(c + 1) * P, 0:D // 2], y[c][:, 0:D // 2]).then_inc(out_done, 16)

        @block.vector
        def _(dve):
            step = Steps(dve, v_step)

            def split(G, p):
                q = p + LEAD
                if isinstance(G, int) and G * NP + q >= G_END * NP:
                    return
                dve.wait_ge(hi_ok, G * NP + (q + 1))
                dve.tensor_tensor(w_lo[:, q % SPL, :, :], raw[:, q % RAW, :, :], w_hi[:, q % SPL, :, :],
                                  ALU.subtract).then_inc(lo_ok, 1)

            def group(G, tasks, take, first=0):
                for p in range(NP):
                    if p >= first:
                        split(G, p)
                    for f in tasks.get(p, ()):
                        f()
                for c in range(4):
                    wait_bank(dve, G, c)
                    take(c)

            def head(H, X, nx, step, slot, slots, q_tile, k_tile, g_tile):
                q, k = feat[:, q_tile, :], feat[:, k_tile, :]

                def halves(ap, s):
                    v = ap.rearrange("p (b two s) -> p b two s", two=2, s=s)
                    return v[:, :, 0, :], v[:, :, 1, :]

                def arg(l):
                    s = LV[l - 1]
                    bk, bq = halves(bcum[:, :], s)
                    ek, eq = halves(ex[EXL[l]][:, :], s)
                    ref = bk[:, :, s - 1:s].to_broadcast([P, T // (2 * s), s])
                    step(dve.tensor_tensor(ek, ref, bk, ALU.subtract))
                    step(dve.tensor_tensor(eq, bq, ref, ALU.subtract))
                    dve.sem_inc(arg_ok, 1)

                def scale(l):
                    s = LV[l - 1]
                    dve.wait_ge(exp_ok, H * NEXP + (4 + l))
                    step(dve.tensor_tensor(kl[l % 2][:, :], k, ex[EXL[l]][:, :], ALU.mult))
                    _, qh = halves(q, s)
                    _, eq = halves(ex[EXL[l]][:, :], s)
                    step(dve.tensor_tensor(ql[l % 2][:, 0:T // 2].rearrange("p (b s) -> p b s", s=s), qh, eq, ALU.mult))
                    dve.sem_inc(lvl_ok, 1)

                def scores(l):
                    dve.wait_ge(sc_ps, H * NL + (l + 1))
                    dve.sem_inc(sc_seen, 1)
                    if l == 0:
                        step(dve.copy_predicated(
                            att[:, :].rearrange("p (c n) -> p c n", c=NT),
                            mask0[:, :].rearrange("p (o n) -> p o n", o=1).to_broadcast([P, NT, P]),
                            sc[0][:, :].rearrange("p (c n) -> p c n", c=NT)))
                    else:
                        s = LV[l - 1]
                        _, a = halves(att[:, :], s)
                        step(dve.copy_predicated(a, maskl[l - 1][:, :].rearrange("p (b s) -> p b s", s=s),
                                                 sc[l % 2][:, 0:T // 2].rearrange("p (b s) -> p b s", s=s)))
                    dve.sem_inc(sc_ok, 1)

                def args():
                    if nx == 1:
                        dve.wait_ge(g_ok, X - 7)
                    step(dve.tensor_tensor_scan(bcum[:, :], reset[:, :], gdec[:, :] if nx == 1 else feat[:, g_tile, :],
                                                0.0, ALU.mult, ALU.add))
                    dve.sem_inc(arg_ok, 1)
                    bc = bcum[:, :].rearrange("p (c n) -> p c n", c=NT)[:, 0:3, :]
                    step(dve.tensor_tensor(ex[2][:, 0:3 * P].rearrange("p (c n) -> p c n", c=3),
                                           bc[:, :, P - 1:P].to_broadcast([P, 3, P]), bc, ALU.subtract))
                    dve.sem_inc(arg_ok, 1)
                    b4 = bcum[:, :].rearrange("p (b r) -> p b r", r=4)
                    step(dve.tensor_tensor(mid, b4[:, :, 1], b4[:, :, 2], ALU.add))
                    step(dve.scalar_tensor_tensor(out=ex[0][:, :].rearrange("p (b r) -> p b r", r=4),
                                                  in0=mid.rearrange("p (b o) -> p b o", o=1).to_broadcast([P, P, 4]),
                                                  scalar=-0.5, in1=b4, op0=ALU.mult, op1=ALU.add))
                    dve.sem_inc(arg_ok, 1)

                def early():
                    if nx == 1:
                        dve.wait_ge(k_ok, X - 7)
                    dve.wait_ge(exp_ok, H * NEXP + 1)
                    step(dve.tensor_tensor(kd[:, :], k[:, 0:3 * P], ex[2][:, 0:3 * P], ALU.mult))
                    dve.sem_inc(kd_ok, 1)
                    arg(1)
                    dve.wait_ge(exp_ok, H * NEXP + 2)
                    step(dve.tensor_tensor(qe[slot][:, :], q[:, P:T], ex[3][:, 0:3 * P], ALU.mult))
                    step(dve.tensor_copy(dec[:, :], ex[3][:, 0:2 * P].rearrange("p (c n) -> p c n", c=2)[:, :, P - 1]))
                    dve.wait_ge(exp_ok, H * NEXP + 3)
                    step(dve.tensor_tensor(kl[0][:, :], k, ex[1][:, :], ALU.mult))
                    dve.wait_ge(exp_ok, H * NEXP + 4)
                    step(dve.tensor_tensor(ql[0][:, :], q, ex[0][:, :], ALU.mult))
                    dve.sem_inc(lvl_ok, 1)
                    arg(2)

                def states(xx):
                    def f():
                        dve.wait_ge(u_ps, X + (xx + 1))
                        step(dve.tensor_copy(state[:, 0:P], st[:, 0:P]))
                        for c in (1, 2):
                            step(dve.scalar_tensor_tensor(out=state[:, c * P:(c + 1) * P], in0=state[:, (c - 1) * P:c * P],
                                                          scalar=dec[:, c - 1:c], in1=st[:, c * P:(c + 1) * P],
                                                          op0=ALU.mult, op1=ALU.add))
                        dve.sem_inc(s_ok, 1)
                    return f

                def norm():
                    dve.wait_ge(rstd_ok, H + 1)
                    for xx in range(nx):
                        o = feat[:, q_tile + xx, :]
                        step(dve.scalar_tensor_tensor(out=o, in0=o, scalar=par[:, bass.ds(X + (R_GNW + xx), 1)],
                                                      in1=sq[:, :], op0=ALU.mult, op1=ALU.mult))

                def on(f, *ls):
                    return [lambda l=l: f(l) for l in ls]

                return dict(args=args, early=early, norm=norm, states=states, arg=lambda l: on(arg, l)[0],
                            scale=lambda l: on(scale, l)[0], scores=lambda l: on(scores, l)[0])

            for j, v in enumerate((EPS * 2.0 ** -LN_SHIFT, -0.5 * LN_SHIFT * LN2, EPS, 1.0)):
                step(dve.memset(cst[:, j:j + 1], v))
            dve.sem_inc(cst_ok, 1)

            def normalise(t):
                dve.wait_ge(xss, t + 1)
                step(dve.reciprocal(rs[:, t:t + 1], rs[:, t:t + 1]))
                step(dve.scalar_tensor_tensor(out=xin[:, t, :], in0=xin[:, t, :], scalar=rs[:, t:t + 1], in1=nwb,
                                              op0=ALU.mult, op1=ALU.mult))
                dve.sem_inc(xn_ok, 1)

            def lows(t):
                for j in range(4):
                    dve.wait_ge(xt_hi, 4 * t + j + 1)
                    h = (slice(None), slice(4 * j, 4 * j + 4), slice(t * P, (t + 1) * P))
                    dve.tensor_tensor(h_lo[h], side[j][:, :].rearrange("p (a n) -> p a n", a=4), h_hi[h],
                                      ALU.subtract).then_inc(xt_lo, 1)

            dve.wait_ge(nb_ok, 4)
            normalise(0)
            split(0, -3)
            split(0, -2)
            lows(0)
            normalise(1)
            split(0, -1)
            split(0, 0)
            lows(1)
            normalise(2)
            lows(2)
            normalise(3)
            lows(3)
            dve.wait_ge(lrw_hi, 1)
            step(dve.tensor_tensor(lrw[:, :, LOWRANK:], lr_raw, lrw[:, :, 0:LOWRANK], ALU.subtract))
            dve.sem_inc(lrw_ok, 1)

            def values(half):
                def f(c):
                    dve.tensor_copy(val[:, c, bass.ds(half * GW, GW)], main[c][:, :]).then_inc(free[c], 1)
                return f

            group(0, {}, values(0), 1)
            dve.wait_ge(par_ps, 1)
            step(dve.tensor_copy(par[:, :], po[:, 0:R_END]))
            l0, l1 = par[:, 0:HG_H], par[:, HG_H:2 * HG_H]
            step(dve.tensor_tensor(lb[:, :], l0, l1, ALU.max))
            step(dve.tensor_tensor(lbt[:, 0:HG_H], l0, lb[:, :], ALU.subtract))
            step(dve.tensor_tensor(lbt[:, HG_H:2 * HG_H], l1, lb[:, :], ALU.subtract))
            dve.sem_inc(lb_arg, 1)
            dve.wait_ge(lb_e, 1)
            step(dve.tensor_tensor(oml[:, :], lbt[:, 0:HG_H], lbt[:, HG_H:2 * HG_H], ALU.add))
            step(dve.reciprocal(oml[:, :], oml[:, :]))
            step(dve.tensor_tensor(lb[:, :], lbt[:, 0:HG_H], oml[:, :], ALU.mult))
            step(dve.tensor_scalar(oml[:, :], lb[:, :], -1.0, 1.0, ALU.mult, ALU.add))
            step(dve.tensor_scalar(noml[:, :], lb[:, :], 1.0, -1.0, ALU.mult, ALU.add))
            step(dve.tensor_scalar(lb[:, :], lb[:, :], LB_MIN, None, ALU.max))
            dve.sem_inc(lb_ok, 1)
            dve.wait_ge(consts, 2)

            def decays():
                for h, bank in enumerate(side):
                    dve.wait_ge(z_abs, h + 1)
                    step(dve.tensor_scalar(gdec[:, :], bank[:, :], par[:, R_BUP + h:R_BUP + h + 1], 0.0, ALU.add, ALU.min))
                    g = feat[:, T_GA + h, :]
                    step(dve.tensor_tensor(g, gdec[:, :], ex[2 + h % 2][:, :], ALU.subtract))
                    dve.sem_inc(z_ok, 1)
                    step(dve.tensor_scalar(g, g, 1.0 / TAU, G_MIN, ALU.mult, ALU.max))

            group(1, {5: [decays]}, values(1))
            group(G_A, {}, lambda c: None)
            group(G_A + 1, {}, lambda c: None)

            def gla_steps(H, stp):
                h = head(H, H * 2, 2, stp, 0, None, H * 2, H * 2 + 1, H + T_GA)
                ar, sl, cp = h["arg"], h["scale"], h["scores"]
                return {0: [h["args"], h["early"]], 1: [sl(1), ar(3), cp(0), sl(2), ar(4)],
                        2: [cp(1), sl(3), ar(5), cp(2), sl(4), h["states"](0), cp(3), sl(5)],
                        3: [cp(4), cp(5)], 5: [h["states"](1)], 6: [h["norm"]]}

            with dve.Fori(0, 2) as i:
                stp = Steps(dve, v_c, i, V_C)
                group(i * 2 + G_C, gla_steps(i * 2, stp), lambda c: None)
                group(i * 2 + (G_C + 1), gla_steps(i * 2 + 1, stp), lambda c: None)
                stp.check()

            def hg_head(m, u, stp):
                return head(m + (GLA_H + u), m + (8 + u), 1, stp, u % 2, None, m + (T_HQ + u), m + (T_HF + u), None)

            def hg_pair(m, stp, more=True):
                hs = [hg_head(m, u, stp) for u in range(3 if more else 2)]
                todo = {}
                for u in range(2):
                    h, nxt, z = hs[u], hs[u + 1:u + 2], 4 * u
                    ar, sl, cp = h["arg"], h["scale"], h["scores"]
                    todo[z] = [sl(1), ar(3), cp(0), sl(2), ar(4)]
                    todo[z + 1] = [cp(1), sl(3), ar(5), cp(2), h["states"](0), sl(4)]
                    todo[z + 2] = [cp(3), sl(5)] + [x["args"] for x in nxt] + [cp(4), cp(5)]
                    todo[z + 3] = [x["early"] for x in nxt] + [h["norm"]]
                return todo

            def gates(e):
                def f(c):
                    dve.wait_ge(gate_ok, e * 4 + (c + 1))
                    o = feat[:, e * 4 + c, :]
                    dve.tensor_tensor(o, o, main[c][:, :], ALU.mult).then_inc(free[c], 1)
                return f

            h0 = hg_head(0, 0, step)
            group(G_D, {4: [h0["args"], h0["early"]]}, values(0))
            group(G_D + 1, hg_pair(0, step), values(1))
            with dve.Fori(0, 2) as i:
                stp = Steps(dve, v_e, i, V_E)
                group(i + G_E, hg_pair(i * 2 + 2, stp), gates(i))
                stp.check()
            group(G_E + 2, hg_pair(6, step, False), gates(2))
            group(G_E + 3, {}, gates(3))
            for k in range(KT):
                dve.wait_ge(mix_hi, k + 1)
                dve.tensor_tensor(h_lo[:, k, :], feat[:, k, :], h_hi[:, k, :], ALU.subtract).then_inc(mix_lo, 1)

            def residual(i):
                def f(c):
                    dve.wait_ge(x2_in, 16 * NT)
                    o = y[c][:, bass.ds(i * GW, GW)]
                    dve.tensor_tensor(o, o, main[c][:, :], ALU.add).then_inc(free[c], 1)
                return f

            with dve.Fori(0, 3) as i:
                group(i + G_F, {}, residual(i))

            def weigh(c):
                def f():
                    dve.wait_ge(fn_in, 16)
                    dve.wait_ge(y_sq, 12)
                    step(dve.tensor_tensor(y[c][:, 0:3 * GW], y[c][:, 0:3 * GW], fnb[:, 0:3 * GW], ALU.mult))
                return f

            for p in range(NP):
                split(G_F + 3, p)
                if 1 <= p <= NT:
                    weigh(p - 1)()
            for c in range(NT):
                wait_bank(dve, G_F + 3, c)
                residual(3)(c)
                dve.wait_ge(yss, c + 1)
                step(dve.tensor_reduce(rsum[:, c:c + 1], rs[:, 4 * c:4 * c + 4], mybir.AxisListType.X, ALU.add))
                dve.sem_inc(ysum, 1)
                step(dve.tensor_tensor(y[c][:, 3 * GW:], y[c][:, 3 * GW:], fnb[:, 3 * GW:], ALU.mult))
                dve.wait_ge(yrt, c + 1)
                step(dve.reciprocal(rsum[:, c:c + 1], rsum[:, c:c + 1]))
                dve.sem_inc(y_fn, 1)
                dve.tensor_scalar(y[c][:, D // 2:], y[c][:, D // 2:], rsum[:, c:c + 1], None, ALU.mult).then_inc(yn, 1)


def kernel(x, norm_w, w_in, gla_w_up, gla_b_up, gla_norm_w, hgrn_lb_logits, hgrn_norm_w, w_out, final_norm_w):
    import numpy as np
    import concourse.bacc as bacc
    from concourse.bass_utils import run_bass_kernel_spmd

    given = {
        "x": np.asarray(x).reshape(T, D), "norm_w": np.asarray(norm_w).reshape(D),
        "w_in": np.asarray(w_in)[0], "gla_w_up": np.asarray(gla_w_up)[0],
        "gla_b_up": np.asarray(gla_b_up).reshape(GLA_H, P), "gla_norm_w": np.asarray(gla_norm_w).reshape(8, P),
        "lb_logits": np.asarray(hgrn_lb_logits).reshape(2 * HG_H, P),
        "hgrn_norm_w": np.asarray(hgrn_norm_w).reshape(HG_H, P), "w_out": np.asarray(w_out)[0],
        "final_norm_w": np.asarray(final_norm_w),
    }
    nc = bacc.Bacc("TRN2", target_bir_lowering=False, num_devices=1)
    arrays, args = {}, {}
    for name, a in given.items():
        a = np.ascontiguousarray(a)
        arrays[f"in_{name}"] = a
        args[name] = nc.dram_tensor(f"in_{name}", a.shape, mybir.dt.from_np(a.dtype), kind="ExternalInput").ap()
    args["out"] = nc.dram_tensor("out_y", (T, D), F32, kind="ExternalOutput").ap()
    hymba_kernel(nc, **args)
    r = run_bass_kernel_spmd(nc, [arrays], core_ids=[0])
    return r.results[0]["out_y"].reshape(1, T, D)
```

```python
from contextlib import ExitStack

import concourse.bass as bass
from concourse import mybir

ALU = mybir.AluOpType
ACT = mybir.ActivationFunctionType
F32 = mybir.dt.float32
F32R = mybir.dt.float32r
U8 = mybir.dt.uint8

P = 128
T = 512
D = 2048
NT = T // P
KT = D // P
GLA_H, HG_H = 4, 8
LOWRANK = 16
TAU = 16.0
EPS = 1e-6
SCALE = float(P) ** -0.5
GW = 512
PK = 2
NP = KT // PK
RAW, SPL = 2, 4
LEAD = 3

C_GQ, C_GK, C_GV, C_GG = 0, 512, 1024, 2048
C_LR = 3072
C_HQ, C_HF, C_HI, C_HG = 3088, 4112, 5136, 6160
G_V, G_A, G_C, G_D, G_E, G_F, G_END = 0, 2, 4, 8, 10, 14, 18
HP = NP // 2
LNEXP = "natural_log_exp_and_others"

LV = [4, 8, 16, 32, 64]
NL = 1 + len(LV)
NEXP = 3 + len(LV) + 1
NARG = 3 + len(LV)
R_LOG, R_BUP, R_GNW, R_HNW, R_END = 0, 16, 20, 28, 36
T_HQ, T_HF, T_GA = 8, 16, 20
LN_SHIFT = 2
G_MIN = -50.0
LB_MIN = 2.0 ** -60
EXL = [None, 2, 3, 0, 1, 3]
LN2 = 0.6931471805599453


class Steps:

    def __init__(self, eng, sem, i=0, per=0):
        self.eng, self.sem, self.i, self.per, self.n = eng, sem, i, per, 0

    def __call__(self, ins):
        self.n += 1
        ins.then_inc(self.sem, 1)
        self.eng.wait_ge(self.sem, self.i * self.per + self.n)
        return ins


def hymba_kernel(nc, x, norm_w, w_in, gla_w_up, gla_b_up, gla_norm_w, lb_logits, hgrn_norm_w, w_out,
                 final_norm_w, out):
    with ExitStack() as ctx:
        def sb(name, shape, dt=F32):
            return ctx.enter_context(nc.sbuf_tensor(name, shape, dt))

        def ps(name):
            return ctx.enter_context(nc.psum_tensor(name, [P, 512], F32))

        def sem(name):
            return ctx.enter_context(nc.semaphore(name))

        h_hi = sb("h_hi", [P, KT, T], F32R)
        h_lo = sb("h_lo", [P, KT, T], F32R)
        raw = sb("raw", [P, RAW, PK, GW])
        w_hi = sb("w_hi", [P, SPL, PK, GW], F32R)
        w_lo = sb("w_lo", [P, SPL, PK, GW], F32R)
        feat = sb("feat", [P, 24, T])
        val = sb("val", [P, NT, 1024])
        bcum = sb("bcum", [P, T])
        gdec = sb("gdec", [P, T])
        ex = [sb(f"ex{i}", [P, T]) for i in range(4)]
        kl = [sb(f"kl{i}", [P, T]) for i in range(2)]
        ql = [sb("ql0", [P, T]), sb("ql1", [P, T // 2])]
        kd = sb("kd", [P, 3 * P])
        kdT = sb("kdT", [P, 3 * P])
        qe = [sb(f"qe{i}", [P, 3 * P]) for i in range(2)]
        att = sb("att", [P, T])
        state = sb("state", [P, 3 * P])
        vst = [sb(f"vst{i}", [P, NT, P]) for i in range(2)]
        sq_lo = sb("sq_lo", [P, T], F32R)
        dec = sb("dec", [P, 2])
        lrw = sb("lrw", [P, KT, 2 * LOWRANK], F32R)
        reset = sb("reset", [P, T], U8)
        mask0 = sb("mask0", [P, P], U8)
        maskl = [sb(f"mask{s}", [P, T // 2], U8) for s in LV[:-1]]
        ones_r = sb("ones_r", [P, P], F32R)
        ident = sb("ident", [P, P])
        par = sb("par", [P, R_END])
        lb = sb("lb", [P, HG_H])
        oml = sb("oml", [P, HG_H])
        noml = sb("noml", [P, HG_H])
        lbt = sb("lbt", [P, 2 * HG_H])
        cst = sb("cst", [P, 4])
        rsum = sb("rsum", [P, NT])
        rs = sb("rs", [P, 4 * NT])

        main = [ps(f"main{c}") for c in range(4)]
        sc = [ps("sc0"), ps("sc1")]
        po = ps("po")
        st = ps("st")
        side = [sc[0], sc[1], po, st]

        xin = feat[:, 0:16, :].rearrange("p (t a) n -> p t (a n)", t=NT)
        nwb = feat[:, 16:20, :].rearrange("p a n -> p (a n)")
        nrow = val[0:1, 0:2, :].rearrange("p a n -> p (a n)")
        mid = kd[:, 0:P]
        ones = kd[:, 0:P]
        sq_hi = lrw.rearrange("p k r -> p (k r)")
        junk = feat[:, 20:24, :].rearrange("p a n -> p (a n)")
        lr_raw = bcum[:, 0:KT * LOWRANK].rearrange("p (k r) -> p k r", k=KT)
        wup = ex[1]
        lr3 = sq_lo
        wup3 = sq_hi
        prow = ex[3]
        y = [val[:, 0:2, :].rearrange("p a n -> p (a n)"), val[:, 2:4, :].rearrange("p a n -> p (a n)"),
             feat[:, 16:20, :].rearrange("p a n -> p (a n)"), feat[:, 20:24, :].rearrange("p a n -> p (a n)")]
        fnb = feat[:, 0:4, :].rearrange("p a n -> p (a n)")
        fjunk = feat[:, 4:5, :].rearrange("p a n -> p (a n)")

        x_in = [sem(f"x_in{t}") for t in range(NT)]
        nw_in = sem("nw_in")
        par_in = sem("par_in")
        lr_in = sem("lr_in")
        up_in = sem("up_in")
        raw_in = [sem(f"raw_in{s}") for s in range(RAW)]
        x2_in = sem("x2_in")
        fn_in = sem("fn_in")
        out_done = sem("out_done")
        consts = sem("consts")
        cst_ok, ones_ok, onesr_ok = sem("cst_ok"), sem("ones_ok"), sem("onesr_ok")
        a_step, v_step, p_step = sem("a_step"), sem("v_step"), sem("p_step")
        lb_arg, z_ok, k_ok, y_fn, ysum, yrt = (sem(n) for n in ("lb_arg", "z_ok", "k_ok", "y_fn", "ysum", "yrt"))
        mid_ok, ln_ok, s_step, norm_ok = sem("mid_ok"), sem("ln_ok"), sem("s_step"), sem("norm_ok")
        sc_seen = sem("sc_seen")
        xss = sem("xss")
        xn_ok = sem("xn_ok")
        xt_ps, xt_hi, xt_lo = sem("xt_ps"), sem("xt_hi"), sem("xt_lo")
        par_ps = sem("par_ps")
        lb_e = sem("lb_e")
        lrw_hi, lrw_ok, lr_ps, lr_ok = sem("lrw_hi"), sem("lrw_ok"), sem("lr_ps"), sem("lr_ok")
        lr_hi = sem("lr_hi")
        z_ps, z_abs = sem("z_ps"), sem("z_abs")
        hi_ok, lo_ok, piece_done = sem("hi_ok"), sem("lo_ok"), sem("piece_done")
        full = sem("full")
        free = [sem(f"free{c}") for c in range(4)]
        g_ok = sem("g_ok")
        gate_ok = sem("gate_ok")
        nb_ps, nb_ok, nb_ok_act, y_sq = sem("nb_ps"), sem("nb_ok"), sem("nb_ok_act"), sem("y_sq")
        arg_ok, exp_ok, kd_ok = sem("arg_ok"), sem("exp_ok"), sem("kd_ok")
        kT_ps, kT_ok, v_ok = sem("kT_ps"), sem("kT_ok"), sem("v_ok")
        lvl_ok, sc_ps, sc_ok = sem("lvl_ok"), sem("sc_ps"), sem("sc_ok")
        u_ps, s_ok, o_ps = sem("u_ps"), sem("s_ok"), sem("o_ps")
        sq_ok, ms_ps, rstd_ok = sem("sq_ok"), sem("ms_ps"), sem("rstd_ok")
        sq_cut, o_ok = sem("sq_cut"), sem("o_ok")
        mix_hi, mix_lo = sem("mix_hi"), sem("mix_lo")
        yss, yn = sem("yss"), sem("yn")

        def wait_bank(eng, G, c):
            if c < 3:
                eng.wait_ge(full, G * 3 + (c + 1))
            else:
                eng.wait_ge(piece_done, G * NP + NP)

        def ms_bank(nx):
            return sc[0] if nx == 2 else po

        block = ctx.enter_context(nc.Block())

        @block.sync
        def _(sp):
            def group(src, col, G, pieces=range(NP)):
                for p in pieces:
                    n = NP * G + p
                    s = p % RAW
                    if not (isinstance(n, int) and n < RAW):
                        sp.wait_ge(lo_ok, n - RAW + 1)
                    rows = src[p * PK * P:(p + 1) * PK * P, bass.ds(col, GW)]
                    sp.dma_start(raw[:, s, :, :], rows.rearrange("(k p) n -> p k n", p=P)).then_inc(raw_in[s], 16)

            sp.dma_start(nrow, norm_w.rearrange("(o n) -> o n", o=1)).then_inc(nw_in, 16)
            def x_tile(t):
                sp.dma_start(xin[:, t, :], x[t * P:(t + 1) * P, :]).then_inc(x_in[t], 16)

            x_tile(0)
            group(w_in, C_GV, G_V, range(0, 2))
            x_tile(1)
            group(w_in, C_GV, G_V, range(2, 4))
            x_tile(2)
            x_tile(3)
            group(w_in, C_GV, G_V, range(4, NP))
            group(w_in, C_GV + GW, G_V + 1)
            with sp.Fori(0, 2) as i:
                group(w_in, i * GW + C_GQ, i + G_A)
            with sp.Fori(0, 2) as i:
                group(w_in, i * GW + C_HQ, i * 2 + G_C)
                group(w_in, i * GW + C_HF, i * 2 + (G_C + 1))
            with sp.Fori(0, 2) as i:
                group(w_in, i * GW + C_HI, i + G_D)
            with sp.Fori(0, 2) as i:
                group(w_in, i * GW + C_GG, i + G_E)
            with sp.Fori(0, 2) as i:
                group(w_in, i * GW + C_HG, i + (G_E + 2))
            group(w_out, 0, G_F, range(LEAD + 1))
            sp.wait_ge(mix_lo, KT)
            for t in range(NT):
                group(w_out, 0, G_F, [LEAD + 1 + t])
                sp.dma_start(y[t], x[t * P:(t + 1) * P, :]).then_inc(x2_in, 16)
            sp.dma_start(fnb, final_norm_w.partition_broadcast(P)).then_inc(fn_in, 16)
            with sp.Fori(0, 3) as i:
                group(w_out, i * GW + GW, i + (G_F + 1))
            for t in range(NT):
                sp.wait_ge(yn, t + 1)
                sp.dma_start(out[t * P:(t + 1) * P, D // 2:], y[t][:, D // 2:]).then_inc(out_done, 16)
            sp.wait_ge(out_done, 2 * 16 * NT)

        @block.gpsimd
        def _(pool):
            n = [0]

            def step(ins):
                n[0] += 1
                ins.then_inc(p_step, 1)
                pool.wait_ge(p_step, n[0])

            step(pool.memset(ones, 1.0))
            pool.sem_inc(ones_ok, 1)
            step(pool.memset(ident[:, :], 0.0))
            step(pool.affine_select(out=ident[:, :], in_=ident[:, :], compare_op=ALU.not_equal, fill=1.0, base=0,
                                    pattern=[[-1, P]], channel_multiplier=1))
            pool.sem_inc(consts, 1)
            step(pool.memset(reset[:, :], 1.0))
            step(pool.memset(reset[:, :].rearrange("p (c n) -> p c n", c=NT)[:, :, 0:1], 0.0))
            m = gdec[:, 0:P]
            step(pool.memset(m[:, :], 1.0))
            step(pool.affine_select(out=m[:, :], in_=m[:, :], compare_op=ALU.is_ge, fill=0.0, base=0,
                                    pattern=[[-4, P // 4], [0, 4]], channel_multiplier=1))
            step(pool.affine_select(out=m[:, :], in_=m[:, :], compare_op=ALU.is_ge, fill=0.0, base=0,
                                    pattern=[[4, P // 4], [1, 4]], channel_multiplier=-1))
            step(pool.tensor_copy(mask0[:, :], m[:, :]))
            for s, mk in zip(LV, maskl):
                m = gdec[:, 0:T // 2]
                step(pool.memset(m, 1.0))
                step(pool.affine_select(out=m, in_=m, compare_op=ALU.is_ge, fill=0.0, base=0,
                                        pattern=[[0, NT], [-2 * s, P // (2 * s)], [0, s]], channel_multiplier=1))
                step(pool.affine_select(out=m, in_=m, compare_op=ALU.is_ge, fill=0.0, base=s - 1,
                                        pattern=[[0, NT], [2 * s, P // (2 * s)], [0, s]], channel_multiplier=-1))
                step(pool.tensor_copy(mk[:, :], m))
            step(pool.memset(att[:, :], 0.0))
            step(pool.memset(kl[1][:, :], 0.0))
            pool.sem_inc(consts, 1)

        @block.tensor
        def _(pe):
            def products(p, c, tokens_stationary):
                s = p % SPL
                cs = slice(c * P, (c + 1) * P)
                for kk in range(PK):
                    k = p * PK + kk
                    if tokens_stationary:
                        pairs = [(h_hi[:, k, cs], w_hi[:, s, kk, :]), (h_hi[:, k, cs], w_lo[:, s, kk, :]),
                                 (h_lo[:, k, cs], w_hi[:, s, kk, :])]
                    else:
                        pairs = [(w_hi[:, s, kk, cs], h_hi[:, k, :]), (w_hi[:, s, kk, cs], h_lo[:, k, :]),
                                 (w_lo[:, s, kk, cs], h_hi[:, k, :])]
                    for j, (a, b) in enumerate(pairs):
                        mm = pe.matmul(main[c][:, :], a, b, start=(k == 0 and j == 0), stop=(k == KT - 1 and j == 2))
                if c == 3:
                    mm.then_inc(piece_done, 1)
                elif p == NP - 1:
                    mm.then_inc(full, 1)

            def group(G, tokens_stationary, tasks=None, pieces=range(NP), before=lambda p: None):
                tasks = tasks or {}
                for p in pieces:
                    before(p)
                    pe.wait_ge(lo_ok, G * NP + (p + 1))
                    for c in range(4):
                        if p == 0:
                            pe.wait_ge(free[c], G * 1)
                        products(p, c, tokens_stationary)
                        for f in tasks.get(4 * p + c, ()):
                            f()

            def by_tile(G, pieces, before=lambda p, c: None, after=lambda p, c: None):
                for c in range(4):
                    for p in pieces:
                        if c == 0:
                            pe.wait_ge(lo_ok, G * NP + (p + 1))
                        before(p, c)
                        products(p, c, True)
                        after(p, c)

            def head_tasks(H, X, nx, at):
                def transposes():
                    pe.wait_ge(kd_ok, H + 1)
                    for c in range(3):
                        mm = pe.transpose(st[:, c * P:(c + 1) * P], kd[:, c * P:(c + 1) * P], ident[:, :])
                    mm.then_inc(kT_ps, 1)

                def level(l):
                    def f():
                        pe.wait_ge(lvl_ok, H * NL + (l + 1))
                        if l >= 2:
                            pe.wait_ge(sc_ok, H * NL + (l - 1))
                        w = P if l == 0 else P // 2
                        m = P // 2 if l == NL - 1 else P
                        for c in range(NT):
                            mm = pe.matmul(sc[l % 2][0:m, c * w:(c + 1) * w], kl[l % 2][:, c * P:c * P + m],
                                           ql[l % 2][:, c * w:(c + 1) * w], start=True, stop=True)
                        mm.then_inc(sc_ps, 1)
                    return f

                def update(xx):
                    def f():
                        if xx == 0:
                            pe.wait_ge(kT_ok, H + 1)
                        pe.wait_ge(v_ok, X + (xx + 1))
                        for c in range(3):
                            mm = pe.matmul(st[:, c * P:(c + 1) * P], kdT[:, c * P:(c + 1) * P], vst[vs(xx)][:, c, :],
                                           start=True, stop=True)
                        mm.then_inc(u_ps, 1)
                    return f

                def outputs(xx):
                    def f():
                        pe.wait_ge(sc_ok, H * NL + NL)
                        pe.wait_ge(s_ok, X + (xx + 1))
                        if nx == 1:
                            pe.wait_ge(norm_ok, X * 1)
                        for c in range(NT):
                            cs = slice(c * P, (c + 1) * P)
                            mm = pe.matmul(po[:, cs], vst[vs(xx)][:, c, :], att[:, cs], start=True, stop=(c == 0))
                            if c:
                                before = slice((c - 1) * P, c * P)
                                mm = pe.matmul(po[:, cs], state[:, before], qe[at["slot"]][:, before],
                                               start=False, stop=True)
                        mm.then_inc(o_ps, 1)
                    return f

                def meansq(xx):
                    def f():
                        pe.wait_ge(sq_cut, X + (xx + 1))
                        ms = ms_bank(nx)
                        pe.matmul(ms[:, :], ones_r[:, :], sq_hi, start=(xx == 0), stop=False)
                        mm = pe.matmul(ms[:, :], ones_r[:, :], sq_lo[:, :], start=False, stop=(xx == nx - 1))
                        if xx == nx - 1:
                            mm.then_inc(ms_ps, 1)
                    return f

                def vs(xx):
                    return xx if nx == 2 else at["slot"]

                todo = {}
                todo.setdefault(at["T"], []).append(transposes)
                for l in range(NL):
                    todo.setdefault(at["L"][l], []).append(level(l))
                for xx in range(nx):
                    todo.setdefault(at["U"][xx], []).append(update(xx))
                    todo.setdefault(at["O"][xx], []).append(outputs(xx))
                    todo.setdefault(at["M"][xx], []).append(meansq(xx))
                return todo

            pe.wait_ge(ones_ok, 1)
            pe.wait_ge(nw_in, 16)
            for j in range(4):
                pe.matmul(main[j][:, :], ones[0:1, :], nrow[:, j * 512:(j + 1) * 512], start=True,
                          stop=True).then_inc(nb_ps, 1)
            pe.wait_ge(consts, 1)

            def transposes(t, half):
                pe.wait_ge(xn_ok, 2 * t + half + 1)
                for j in (2 * half, 2 * half + 1):
                    if t:
                        pe.wait_ge(xt_lo, 4 * (t - 1) + j + 1)
                    for k in range(4 * j, 4 * j + 4):
                        mm = pe.transpose(side[j][:, (k % 4) * P:(k % 4 + 1) * P], xin[:, t, k * P:(k + 1) * P],
                                          ident[:, :])
                    mm.then_inc(xt_ps, 1)

            def before(p, c):
                if p == 0 and c % 2 == 0:
                    pe.wait_ge([nb_ok, nb_ok_act][c // 2], 2)
                if p % 2 == 0:
                    pe.wait_ge(xt_lo, 4 * c + p // 2 + 1)

            def after(p, c):
                if p == 1:
                    for t in ([0] if c == 0 else []) + ([c + 1] if c < 3 else []):
                        for half in ([1] if t == 0 else [0, 1]):
                            transposes(t, half)

            def low_rank():
                pe.wait_ge(lrw_ok, 1)
                for k in range(KT):
                    pe.matmul(st[0:2 * LOWRANK, :], lrw[:, k, :], h_hi[:, k, :], start=(k == 0), stop=False)
                    mm = pe.matmul(st[0:2 * LOWRANK, :], lrw[:, k, :], h_lo[:, k, :], start=False, stop=(k == KT - 1))
                mm.then_inc(lr_ps, 1)

            def parameters():
                pe.wait_ge(par_in, 64)
                pe.transpose(po[:, 0:R_END], prow[0:R_END, 0:P], ident[0:R_END, 0:R_END]).then_inc(par_ps, 1)

            def decay_inputs():
                pe.wait_ge(lr_ok, 1)
                for h, bank in enumerate(side):
                    pe.matmul(bank[:, :], wup3[0:6 * LOWRANK, h * P:(h + 1) * P], lr3[0:6 * LOWRANK, :],
                              start=True, stop=True).then_inc(z_ps, 1)

            transposes(0, 0)
            by_tile(0, range(HP), before, after)
            pe.wait_ge(xt_lo, KT)
            group(0, True, {31: [parameters]}, range(HP, NP))
            group(1, True, {8: [low_rank], 16: [decay_inputs]})
            with pe.Fori(0, 2) as i:
                group(i + G_A, False)
            gla_at = dict(slot=0, T=7, L=[9, 11, 12, 14, 15, 17], U=[13, 22], O=[19, 24], M=[22, 27])
            with pe.Fori(0, 2) as i:
                for a in range(2):
                    H = i * 2 + a
                    group(i * 2 + (G_C + a), False, head_tasks(H, H * 2, 2, gla_at))

            def hg_pair(m):
                todo = {}
                for u in range(2):
                    z = 16 * u
                    at = dict(slot=u, T=z, L=[z + q for q in (1, 3, 5, 7, 8, 9)], U=[z + 3], O=[z + 10], M=[z + 14])
                    todo |= head_tasks(m + (GLA_H + u), m + (8 + u), 1, at)
                return todo

            group(G_D, True)
            group(G_D + 1, True, hg_pair(0))
            with pe.Fori(0, 2) as i:
                group(i + G_E, False, hg_pair(i * 2 + 2))
            group(G_E + 2, False, hg_pair(6))
            group(G_E + 3, False)
            group(G_F, True, before=lambda p: pe.wait_ge(mix_lo, PK * (p + 1)))
            with pe.Fori(0, 2) as i:
                group(i + (G_F + 1), True)
            group(G_F + 3, True, pieces=range(HP))
            by_tile(G_F + 3, range(HP, NP))

        @block.scalar
        def _(act):
            step = Steps(act, a_step)

            def split(G, p):
                q = p + LEAD
                if isinstance(G, int) and G * NP + q >= G_END * NP:
                    return
                act.wait_ge(raw_in[q % RAW], G * (NP // RAW * 16) + 16 * (q // RAW + 1))
                if not (isinstance(G, int) and G * NP + q < SPL):
                    act.wait_ge(piece_done, G * NP + (q - SPL + 1))
                act.activation(w_hi[:, q % SPL, :, :], raw[:, q % RAW, :, :], ACT.Copy).then_inc(hi_ok, 1)

            def group(G, tasks, take, first=0):
                for p in range(NP):
                    if p >= first:
                        split(G, p)
                    for f in tasks.get(p, ()):
                        f()
                for c in range(4):
                    wait_bank(act, G, c)
                    take(c)
                for f in tasks.get("end", ()):
                    f()

            def head(H, X, nx, slot, q_tile):
                def e(n_arg, dst, src, scale=1.0):
                    act.wait_ge(arg_ok, H * NARG + n_arg)
                    act.activation(dst, src, ACT.Exp, scale=scale).then_inc(exp_ok, 1)

                def decay():
                    m = X - 8
                    r = feat[:, m + T_HF, :]
                    act.activation(gdec[:, :], r, ACT.Ln, bias=lb[:, bass.ds(m, 1)],
                                   scale=oml[:, bass.ds(m, 1)]).then_inc(g_ok, 1)
                    act.activation(r, r, ACT.Identity, bias=oml[:, bass.ds(m, 1)],
                                   scale=noml[:, bass.ds(m, 1)]).then_inc(k_ok, 1)

                def early():
                    e(2, ex[2][:, 0:3 * P], ex[2][:, 0:3 * P])
                    e(2, ex[3][:, 0:3 * P], bcum[:, P:T])
                    e(3, ex[1][:, :], ex[0][:, :], -1.0)
                    e(3, ex[0][:, :], ex[0][:, :])

                def values():
                    for xx in range(nx):
                        col = (X + xx) * P if nx == 2 else (X - 8) * P
                        act.activation(vst[xx if nx == 2 else slot][:, :, :], val[:, :, bass.ds(col, P)],
                                       ACT.Copy).then_inc(v_ok, 1)

                def level(l):
                    def f():
                        e(3 + l, ex[EXL[l]][:, :], ex[EXL[l]][:, :])
                    return f

                def keys():
                    act.wait_ge(kT_ps, H + 1)
                    act.activation(kdT[:, :], st[:, 0:3 * P], ACT.Copy).then_inc(kT_ok, 1)

                def take(xx):
                    def f():
                        act.wait_ge(o_ps, X + (xx + 1))
                        act.activation(feat[:, q_tile + xx, :], po[:, :], ACT.Copy)
                        act.activation(sq_hi, po[:, :], ACT.Square).then_inc(o_ok, 1)
                        act.wait_ge(o_ok, X + (xx + 1))
                        act.activation(po[:, :], po[:, :], ACT.Square).then_inc(sq_ok, 1)
                    return f

                def rstd():
                    act.wait_ge(ms_ps, H + 1)
                    ms = ms_bank(nx)
                    act.activation(ms[:, :], ms[:, :], ACT.Ln, bias=cst[:, 0:1],
                                   scale=2.0 ** -LN_SHIFT / (P * nx)).then_inc(ln_ok, 1)
                    act.wait_ge(ln_ok, H + 1)
                    act.activation(ms[:, :], ms[:, :], ACT.Exp, bias=cst[:, 1:2], scale=-0.5).then_inc(rstd_ok, 1)

                return dict(decay=decay, early=early, values=values, level=level, keys=keys, take=take, rstd=rstd)

            act.preload_act_table_set("sqrt_and_others")
            act.wait_ge(cst_ok, 1)

            def broadcast(j):
                act.wait_ge(nb_ps, j + 1)
                act.activation(nwb[:, j * 512:(j + 1) * 512], main[j][:, :], ACT.Copy).then_inc(nb_ok_act, 1)

            def squares(t):
                act.wait_ge(x_in[t], 16)
                step(act.activation(junk, xin[:, t, :], ACT.Square, accum_out=rs[:, t:t + 1]))
                step(act.activation(rs[:, t:t + 1], rs[:, t:t + 1], ACT.Sqrt, bias=cst[:, 2:3], scale=1.0 / D))
                act.sem_inc(xss, 1)

            def highs(t, js=range(4)):
                for j in js:
                    act.wait_ge(xt_ps, 4 * t + j + 1)
                    act.activation(h_hi[:, 4 * j:4 * j + 4, t * P:(t + 1) * P],
                                   side[j][:, :].rearrange("p (a n) -> p a n", a=4), ACT.Copy).then_inc(xt_hi, 1)

            squares(0)
            split(0, -3)
            broadcast(2)
            highs(0, [0])
            broadcast(3)
            split(0, -2)
            highs(0, [1])
            squares(1)
            split(0, -1)
            highs(0, [2, 3])
            split(0, 0)
            highs(1)
            squares(2)
            act.dma_start(lr_raw, w_in[:, C_LR:C_LR + LOWRANK].rearrange("(k p) r -> p k r", p=P)).then_inc(lr_in, 16)
            highs(2)
            squares(3)
            for a in range(2):
                act.dma_start(wup[a * LOWRANK:(a + 1) * LOWRANK, :], gla_w_up).then_inc(up_in, 16)
            highs(3)
            act.dma_start(prow[R_LOG:R_BUP, 0:P], lb_logits).then_inc(par_in, 16)
            act.dma_start(prow[R_BUP:R_GNW, 0:P], gla_b_up).then_inc(par_in, 16)
            act.dma_start(prow[R_GNW:R_HNW, 0:P], gla_norm_w).then_inc(par_in, 16)
            act.dma_start(prow[R_HNW:R_END, 0:P], hgrn_norm_w).then_inc(par_in, 16)
            act.wait_ge(lr_in, 16)
            step(act.activation(lrw[:, :, 0:LOWRANK], lr_raw, ACT.Copy))
            act.sem_inc(lrw_hi, 1)
            act.preload_act_table_set(LNEXP)

            def bounds():
                act.wait_ge(lb_arg, 1)
                step(act.activation(lbt[:, :], lbt[:, :], ACT.Exp))
                act.sem_inc(lb_e, 1)

            def low_rank():
                n = 2 * LOWRANK
                act.wait_ge(lr_ps, 1)
                act.wait_ge(up_in, 32)
                act.activation(lr3[0:n, :], st[0:n, :], ACT.Copy)
                act.activation(lr3[2 * n:3 * n, :], st[0:n, :], ACT.Copy)
                act.activation(wup3[n:2 * n, :], wup[0:n, :], ACT.Copy)
                act.activation(wup3[0:n, :], wup[0:n, :], ACT.Copy).then_inc(lr_hi, 1)

            def decays():
                for h, bank in enumerate(side):
                    act.wait_ge(z_ps, h + 1)
                    if h >= 2:
                        act.wait_ge(z_ok, h - 1)
                    t = ex[2 + h % 2][:, :]
                    step(act.activation(t, bank[:, :], ACT.Abs, bias=par[:, R_BUP + h:R_BUP + h + 1]))
                    step(act.activation(t, t, ACT.Exp, scale=-1.0))
                    step(act.activation(t, t, ACT.Ln, bias=cst[:, 3:4]))
                    act.sem_inc(z_abs, 1)

            def store(tile, scale=1.0, func=ACT.Copy):
                def f(c):
                    act.activation(feat[:, tile(c), :], main[c][:, :], func, scale=scale).then_inc(free[c], 1)
                return f

            group(0, {}, lambda c: None, 1)
            group(1, {0: [bounds], 3: [low_rank], 5: [decays]}, lambda c: None)
            group(G_A, {}, store(lambda c: 2 * c, SCALE))
            group(G_A + 1, {}, store(lambda c: 2 * c + 1))

            def gla_steps(H):
                h = head(H, H * 2, 2, 0, H * 2)
                lv = h["level"]
                return {0: [h["early"], h["values"]], 1: [lv(1), h["keys"], lv(2)], 2: [lv(3), lv(4), lv(5)],
                        4: [h["take"](0)], 5: [h["take"](1)], 6: [h["rstd"]]}

            with act.Fori(0, 2) as i:
                group(i * 2 + G_C, gla_steps(i * 2), store(lambda c: i * 4 + (T_HQ + c), SCALE))
                group(i * 2 + (G_C + 1), gla_steps(i * 2 + 1),
                      store(lambda c: i * 4 + (T_HF + c), 1.0, ACT.Sigmoid))
                act.preload_act_table_set(LNEXP)

            def hg_head(m, u):
                return head(m + (GLA_H + u), m + (8 + u), 1, u % 2, m + (8 + u))

            def hg_pair(m, more=True):
                hs = [hg_head(m, u) for u in range(3 if more else 2)]
                todo = {}
                for u in range(2):
                    h, nxt, lv, z = hs[u], hs[u + 1:u + 2], hs[u]["level"], 4 * u
                    todo[z] = [lv(1), h["values"], h["keys"], lv(2)]
                    todo[z + 1] = [lv(3), lv(4)]
                    todo[z + 2] = [lv(5)] + [f for x in nxt for f in (x["decay"], x["early"])] + [h["take"](0)]
                    if u == 0:
                        todo[z + 3] = [h["rstd"]]
                if not (isinstance(m, int) and m == 0):
                    todo["end"] = [lambda: act.preload_act_table_set(LNEXP)]
                todo.setdefault("end", []).append(h["rstd"])
                return todo

            def silu(c):
                act.activation(main[c][:, :], main[c][:, :], ACT.Silu).then_inc(gate_ok, 1)

            h0 = hg_head(0, 0)
            group(G_D, {4: [h0["decay"], h0["early"]]}, lambda c: None)
            for c in range(4):
                act.wait_ge(free[c], G_D + 1)
            group(G_D + 1, hg_pair(0), lambda c: None)
            for c in range(4):
                act.wait_ge(free[c], G_D + 2)
            with act.Fori(0, 2) as i:
                group(i + G_E, hg_pair(i * 2 + 2), silu)
            group(G_E + 2, hg_pair(6, False), silu)

            def mixed(*ks):
                def f():
                    for k in ks:
                        act.wait_ge(free[k % 4], G_E + k // 4 + 1)
                        act.activation(h_hi[:, k, :], feat[:, k, :], ACT.Copy).then_inc(mix_hi, 1)
                return f

            group(G_E + 3, {p: [mixed(2 * p - 2, 2 * p - 1)] for p in range(1, 7)}, silu)
            mixed(*range(12, KT))()

            def out_squares(i, stp):
                def f(c):
                    act.wait_ge(free[c], i + (G_F + 1))
                    stp(act.activation(fjunk, y[c][:, bass.ds(i * GW, GW)], ACT.Square,
                                       accum_out=rs[:, bass.ds(i + 4 * c, 1)]))
                return f

            with act.Fori(0, 3) as i:
                stp = Steps(act, y_sq, i, 4)
                group(i + G_F, {}, out_squares(i, stp))
            for p in range(NP):
                split(G_F + 3, p)
            for c in range(NT):
                act.wait_ge(free[c], G_END)
                step(act.activation(fjunk, y[c][:, 3 * GW:], ACT.Square, accum_out=rs[:, 4 * c + 3:4 * c + 4]))
                act.sem_inc(yss, 1)
                act.wait_ge(ysum, c + 1)
                step(act.activation(rsum[:, c:c + 1], rsum[:, c:c + 1], ACT.Sqrt, bias=cst[:, 2:3], scale=1.0 / D))
                act.sem_inc(yrt, 1)
                act.wait_ge(y_fn, c + 1)
                step(act.activation(y[c][:, 0:D // 2], y[c][:, 0:D // 2], ACT.Copy, scale=rsum[:, c:c + 1]))
                act.dma_start(out[c * P:(c + 1) * P, 0:D // 2], y[c][:, 0:D // 2]).then_inc(out_done, 16)

        @block.vector
        def _(dve):
            step = Steps(dve, v_step)

            def split(G, p):
                q = p + LEAD
                if isinstance(G, int) and G * NP + q >= G_END * NP:
                    return
                dve.wait_ge(hi_ok, G * NP + (q + 1))
                dve.tensor_tensor(w_lo[:, q % SPL, :, :], raw[:, q % RAW, :, :], w_hi[:, q % SPL, :, :],
                                  ALU.subtract).then_inc(lo_ok, 1)

            def group(G, tasks, take, first=0):
                for p in range(NP):
                    if p >= first:
                        split(G, p)
                    for f in tasks.get(p, ()):
                        f()
                for c in range(4):
                    wait_bank(dve, G, c)
                    take(c)
                for f in tasks.get("end", ()):
                    f()

            def head(H, X, nx, slot, q_tile, k_tile, g_tile):
                q, k = feat[:, q_tile, :], feat[:, k_tile, :]

                def halves(ap, s):
                    v = ap.rearrange("p (b two s) -> p b two s", two=2, s=s)
                    return v[:, :, 0, :], v[:, :, 1, :]

                def arg(l):
                    s = LV[l - 1]
                    bk, bq = halves(bcum[:, :], s)
                    ek, eq = halves(ex[EXL[l]][:, :], s)
                    ref = bk[:, :, s - 1:s].to_broadcast([P, T // (2 * s), s])
                    if l == 1:
                        dve.wait_ge(kd_ok, H + 1)
                    else:
                        dve.wait_ge(lvl_ok, H * NL + (3 if l == 5 else 1))
                    dve.tensor_tensor(ek, ref, bk, ALU.subtract)
                    dve.tensor_tensor(eq, bq, ref, ALU.subtract).then_inc(arg_ok, 1)

                def scale(l):
                    s = LV[l - 1]
                    dve.wait_ge(exp_ok, H * NEXP + (4 + l))
                    kh, _ = halves(k, s)
                    _, qh = halves(q, s)
                    ek, eq = halves(ex[EXL[l]][:, :], s)
                    keys, _ = halves(kl[l % 2][:, :], s)
                    dve.tensor_tensor(keys, kh, ek, ALU.mult)
                    dve.tensor_tensor(ql[l % 2][:, 0:T // 2].rearrange("p (b s) -> p b s", s=s), qh, eq,
                                      ALU.mult).then_inc(lvl_ok, 1)

                def scores(l):
                    if l:
                        dve.wait_ge(sc_ok, H * NL + l)
                    dve.wait_ge(sc_ps, H * NL + (l + 1))
                    dve.sem_inc(sc_seen, 1)
                    if l == 0:
                        dve.copy_predicated(
                            att[:, :].rearrange("p (c n) -> p c n", c=NT),
                            mask0[:, :].rearrange("p (o n) -> p o n", o=1).to_broadcast([P, NT, P]),
                            sc[0][:, :].rearrange("p (c n) -> p c n", c=NT)).then_inc(sc_ok, 1)
                    elif l < NL - 1:
                        s = LV[l - 1]
                        _, a = halves(att[:, :], s)
                        got = sc[l % 2][:, 0:T // 2].rearrange("p (b s) -> p b s", s=s)
                        dve.copy_predicated(a, maskl[l - 1][:, :].rearrange("p (b s) -> p b s", s=s),
                                            got).then_inc(sc_ok, 1)
                    else:
                        s = P // 2
                        _, a = halves(att[0:s, :], s)
                        got = sc[l % 2][0:s, 0:T // 2].rearrange("p (b s) -> p b s", s=s)
                        dve.tensor_copy(a, got).then_inc(sc_ok, 1)

                def args():
                    if nx == 1:
                        dve.wait_ge(g_ok, X - 7)
                    dve.tensor_tensor_scan(bcum[:, :], reset[:, :], gdec[:, :] if nx == 1 else feat[:, g_tile, :],
                                           0.0, ALU.mult, ALU.add).then_inc(arg_ok, 1)

                def ends():
                    dve.wait_ge(arg_ok, H * NARG + 1)
                    bc = bcum[:, :].rearrange("p (c n) -> p c n", c=NT)[:, 0:3, :]
                    dve.tensor_tensor(ex[2][:, 0:3 * P].rearrange("p (c n) -> p c n", c=3),
                                      bc[:, :, P - 1:P].to_broadcast([P, 3, P]), bc, ALU.subtract).then_inc(arg_ok, 1)
                    b4 = bcum[:, :].rearrange("p (b r) -> p b r", r=4)
                    dve.tensor_tensor(mid, b4[:, :, 1], b4[:, :, 2], ALU.add).then_inc(mid_ok, 1)
                    dve.wait_ge(mid_ok, H + 1)
                    dve.scalar_tensor_tensor(out=ex[0][:, :].rearrange("p (b r) -> p b r", r=4),
                                             in0=mid.rearrange("p (b o) -> p b o", o=1).to_broadcast([P, P, 4]),
                                             scalar=-0.5, in1=b4, op0=ALU.mult, op1=ALU.add).then_inc(arg_ok, 1)

                def early():
                    if nx == 1:
                        dve.wait_ge(k_ok, X - 7)
                    dve.wait_ge(exp_ok, H * NEXP + 1)
                    dve.wait_ge(arg_ok, H * NARG + 3)
                    dve.tensor_tensor(kd[:, :], k[:, 0:3 * P], ex[2][:, 0:3 * P], ALU.mult).then_inc(kd_ok, 1)
                    arg(1)
                    dve.wait_ge(exp_ok, H * NEXP + 2)
                    dve.tensor_tensor(qe[slot][:, :], q[:, P:T], ex[3][:, 0:3 * P], ALU.mult)
                    dve.tensor_copy(dec[:, :], ex[3][:, 0:2 * P].rearrange("p (c n) -> p c n", c=2)[:, :, P - 1])
                    dve.wait_ge(exp_ok, H * NEXP + 3)
                    dve.tensor_tensor(kl[0][:, :], k, ex[1][:, :], ALU.mult)
                    dve.wait_ge(exp_ok, H * NEXP + 4)
                    dve.tensor_tensor(ql[0][:, :], q, ex[0][:, :], ALU.mult).then_inc(lvl_ok, 1)
                    arg(2)

                def states(xx):
                    def f():
                        dve.wait_ge(u_ps, X + (xx + 1))
                        dve.tensor_copy(state[:, 0:P], st[:, 0:P]).then_inc(s_step, 1)
                        for c in (1, 2):
                            dve.wait_ge(s_step, (X + xx) * 2 + c)
                            dve.scalar_tensor_tensor(out=state[:, c * P:(c + 1) * P], in0=state[:, (c - 1) * P:c * P],
                                                     scalar=dec[:, c - 1:c], in1=st[:, c * P:(c + 1) * P],
                                                     op0=ALU.mult, op1=ALU.add).then_inc(s_step if c == 1 else s_ok, 1)
                    return f

                def cut(xx):
                    def f():
                        dve.wait_ge(sq_ok, X + (xx + 1))
                        dve.tensor_tensor(sq_lo[:, :], po[:, :], sq_hi, ALU.subtract).then_inc(sq_cut, 1)
                    return f

                def norm():
                    dve.wait_ge(rstd_ok, H + 1)
                    for xx in range(nx):
                        o = feat[:, q_tile + xx, :]
                        dve.scalar_tensor_tensor(out=o, in0=o, scalar=par[:, bass.ds(X + (R_GNW + xx), 1)],
                                                 in1=ms_bank(nx)[:, :], op0=ALU.mult, op1=ALU.mult).then_inc(norm_ok, 1)

                def of(f):
                    return lambda l: lambda: f(l)

                return dict(args=args, ends=ends, early=early, norm=norm, states=states, cut=cut, arg=of(arg),
                            scale=of(scale), scores=of(scores))

            for j, v in enumerate((EPS * 2.0 ** -LN_SHIFT, -0.5 * LN_SHIFT * LN2, EPS, 1.0)):
                step(dve.memset(cst[:, j:j + 1], v))
            dve.sem_inc(cst_ok, 1)

            dve.wait_ge(ones_ok, 1)
            dve.tensor_copy(ones_r[:, :], ones).then_inc(onesr_ok, 1)

            def normalise(t, half):
                h = slice(half * D // 2, (half + 1) * D // 2)
                if half == 0:
                    dve.wait_ge(xss, t + 1)
                    step(dve.reciprocal(rs[:, t:t + 1], rs[:, t:t + 1]))
                dve.scalar_tensor_tensor(out=xin[:, t, h], in0=xin[:, t, h], scalar=rs[:, t:t + 1], in1=nwb[:, h],
                                         op0=ALU.mult, op1=ALU.mult).then_inc(xn_ok, 1)

            def lows(t, js=range(4)):
                for j in js:
                    dve.wait_ge(xt_hi, 4 * t + j + 1)
                    h = (slice(None), slice(4 * j, 4 * j + 4), slice(t * P, (t + 1) * P))
                    dve.tensor_tensor(h_lo[h], side[j][:, :].rearrange("p (a n) -> p a n", a=4), h_hi[h],
                                      ALU.subtract).then_inc(xt_lo, 1)

            for j in range(2):
                dve.wait_ge(nb_ps, j + 1)
                dve.tensor_copy(nwb[:, j * 512:(j + 1) * 512], main[j][:, :]).then_inc(nb_ok, 1)
            dve.wait_ge(nb_ok, 2)
            normalise(0, 0)
            split(0, -3)
            lows(0, [0])
            split(0, -2)
            dve.wait_ge(nb_ok_act, 2)
            normalise(0, 1)
            lows(0, [1])
            normalise(1, 0)
            normalise(1, 1)
            split(0, -1)
            lows(0, [2, 3])
            split(0, 0)
            lows(1)
            for t in (2, 3):
                normalise(t, 0)
                normalise(t, 1)
                lows(t)
            dve.wait_ge(lrw_hi, 1)
            step(dve.tensor_tensor(lrw[:, :, LOWRANK:], lr_raw, lrw[:, :, 0:LOWRANK], ALU.subtract))
            dve.sem_inc(lrw_ok, 1)

            def values(half):
                def f(c):
                    dve.tensor_copy(val[:, c, bass.ds(half * GW, GW)], main[c][:, :]).then_inc(free[c], 1)
                return f

            group(0, {}, values(0), 1)
            dve.wait_ge(par_ps, 1)
            step(dve.tensor_copy(par[:, :], po[:, 0:R_END]))
            l0, l1 = par[:, 0:HG_H], par[:, HG_H:2 * HG_H]
            step(dve.tensor_tensor(lb[:, :], l0, l1, ALU.max))
            step(dve.tensor_tensor(lbt[:, 0:HG_H], l0, lb[:, :], ALU.subtract))
            step(dve.tensor_tensor(lbt[:, HG_H:2 * HG_H], l1, lb[:, :], ALU.subtract))
            dve.sem_inc(lb_arg, 1)
            dve.wait_ge(lb_e, 1)
            step(dve.tensor_tensor(oml[:, :], lbt[:, 0:HG_H], lbt[:, HG_H:2 * HG_H], ALU.add))
            step(dve.reciprocal(oml[:, :], oml[:, :]))
            step(dve.tensor_tensor(lb[:, :], lbt[:, 0:HG_H], oml[:, :], ALU.mult))
            step(dve.tensor_scalar(oml[:, :], lb[:, :], -1.0, 1.0, ALU.mult, ALU.add))
            step(dve.tensor_scalar(noml[:, :], lb[:, :], 1.0, -1.0, ALU.mult, ALU.add))
            step(dve.tensor_scalar(lb[:, :], lb[:, :], LB_MIN, None, ALU.max))
            dve.wait_ge(consts, 2)

            def decays():
                for h, bank in enumerate(side):
                    dve.wait_ge(z_abs, h + 1)
                    step(dve.tensor_scalar(gdec[:, :], bank[:, :], par[:, R_BUP + h:R_BUP + h + 1], 0.0, ALU.add,
                                           ALU.min))
                    g = feat[:, T_GA + h, :]
                    step(dve.tensor_tensor(g, gdec[:, :], ex[2 + h % 2][:, :], ALU.subtract))
                    dve.sem_inc(z_ok, 1)
                    step(dve.tensor_scalar(g, g, 1.0 / TAU, G_MIN, ALU.mult, ALU.max))

            def low_rank():
                n = 2 * LOWRANK
                dve.wait_ge(lr_hi, 1)
                dve.tensor_tensor(lr3[n:2 * n, :], st[0:n, :], lr3[0:n, :], ALU.subtract)
                dve.tensor_tensor(wup3[2 * n:3 * n, :], wup[0:n, :], wup3[0:n, :], ALU.subtract).then_inc(lr_ok, 1)

            group(1, {3: [low_rank], 5: [decays]}, values(1))
            group(G_A, {}, lambda c: None)
            group(G_A + 1, {}, lambda c: None)

            def gla_steps(H):
                h = head(H, H * 2, 2, 0, H * 2, H * 2 + 1, H + T_GA)
                ar, sl, cp = h["arg"], h["scale"], h["scores"]
                return {0: [h["args"], h["ends"], h["early"]], 1: [sl(1), ar(3), cp(0), sl(2), ar(4)],
                        2: [cp(1), sl(3), ar(5), cp(2), sl(4), h["states"](0), cp(3), sl(5)],
                        3: [cp(4), cp(5)], 4: [h["cut"](0)], 5: [h["states"](1), h["cut"](1)], 6: [h["norm"]]}

            with dve.Fori(0, 2) as i:
                group(i * 2 + G_C, gla_steps(i * 2), lambda c: None)
                group(i * 2 + (G_C + 1), gla_steps(i * 2 + 1), lambda c: None)

            def hg_head(m, u):
                return head(m + (GLA_H + u), m + (8 + u), 1, u % 2, m + (T_HQ + u), m + (T_HF + u), None)

            def hg_pair(m, more=True):
                hs = [hg_head(m, u) for u in range(3 if more else 2)]
                todo = {}
                for u in range(2):
                    h, nxt, z = hs[u], hs[u + 1:u + 2], 4 * u
                    ar, sl, cp = h["arg"], h["scale"], h["scores"]
                    todo[z] = [sl(1), ar(3), cp(0), sl(2), ar(4)]
                    todo[z + 1] = [cp(1), sl(3), ar(5), cp(2), h["states"](0), sl(4)]
                    todo[z + 2] = ([cp(3), sl(5), cp(4)] + [x["args"] for x in nxt] + [cp(5)]
                                   + [f for x in nxt for f in (x["ends"], x["early"])] + [h["cut"](0)])
                    todo[z + 3 if u == 0 else "end"] = [h["norm"]]
                return todo

            def gates(e):
                def f(c):
                    dve.wait_ge(gate_ok, e * 4 + (c + 1))
                    dve.wait_ge(norm_ok, e * 4 + (c + 1))
                    o = feat[:, e * 4 + c, :]
                    dve.tensor_tensor(o, o, main[c][:, :], ALU.mult).then_inc(free[c], 1)
                return f

            h0 = hg_head(0, 0)
            group(G_D, {4: [h0["args"], h0["ends"], h0["early"]]}, values(0))
            group(G_D + 1, hg_pair(0), values(1))
            with dve.Fori(0, 2) as i:
                group(i + G_E, hg_pair(i * 2 + 2), gates(i))
            group(G_E + 2, hg_pair(6, False), gates(2))

            def mixed(*ks):
                def f():
                    for k in ks:
                        dve.wait_ge(mix_hi, k + 1)
                        dve.tensor_tensor(h_lo[:, k, :], feat[:, k, :], h_hi[:, k, :], ALU.subtract).then_inc(mix_lo, 1)
                return f

            group(G_E + 3, {p: [mixed(2 * p - 2, 2 * p - 1)] for p in range(1, 7)}, gates(3))
            mixed(*range(12, KT))()

            def residual(i):
                def f(c):
                    dve.wait_ge(x2_in, 16 * NT)
                    o = y[c][:, bass.ds(i * GW, GW)]
                    dve.tensor_tensor(o, o, main[c][:, :], ALU.add).then_inc(free[c], 1)
                return f

            with dve.Fori(0, 3) as i:
                group(i + G_F, {}, residual(i))

            def weigh(c):
                def f():
                    dve.wait_ge(fn_in, 16)
                    dve.wait_ge(y_sq, 12)
                    step(dve.tensor_tensor(y[c][:, 0:3 * GW], y[c][:, 0:3 * GW], fnb[:, 0:3 * GW], ALU.mult))
                return f

            for p in range(NP):
                split(G_F + 3, p)
                if 1 <= p <= NT:
                    weigh(p - 1)()
            for c in range(NT):
                wait_bank(dve, G_F + 3, c)
                residual(3)(c)
                dve.wait_ge(yss, c + 1)
                step(dve.tensor_reduce(rsum[:, c:c + 1], rs[:, 4 * c:4 * c + 4], mybir.AxisListType.X, ALU.add))
                dve.sem_inc(ysum, 1)
                step(dve.tensor_tensor(y[c][:, 3 * GW:], y[c][:, 3 * GW:], fnb[:, 3 * GW:], ALU.mult))
                dve.wait_ge(yrt, c + 1)
                step(dve.reciprocal(rsum[:, c:c + 1], rsum[:, c:c + 1]))
                dve.sem_inc(y_fn, 1)
                dve.tensor_scalar(y[c][:, D // 2:], y[c][:, D // 2:], rsum[:, c:c + 1], None, ALU.mult).then_inc(yn, 1)


def kernel(x, norm_w, w_in, gla_w_up, gla_b_up, gla_norm_w, hgrn_lb_logits, hgrn_norm_w, w_out, final_norm_w):
    import numpy as np
    import concourse.bacc as bacc
    from concourse.bass_utils import run_bass_kernel_spmd

    given = {
        "x": np.asarray(x).reshape(T, D), "norm_w": np.asarray(norm_w).reshape(D),
        "w_in": np.asarray(w_in)[0], "gla_w_up": np.asarray(gla_w_up)[0],
        "gla_b_up": np.asarray(gla_b_up).reshape(GLA_H, P), "gla_norm_w": np.asarray(gla_norm_w).reshape(8, P),
        "lb_logits": np.asarray(hgrn_lb_logits).reshape(2 * HG_H, P),
        "hgrn_norm_w": np.asarray(hgrn_norm_w).reshape(HG_H, P), "w_out": np.asarray(w_out)[0],
        "final_norm_w": np.asarray(final_norm_w),
    }
    nc = bacc.Bacc("TRN2", target_bir_lowering=False, num_devices=1)
    arrays, args = {}, {}
    for name, a in given.items():
        a = np.ascontiguousarray(a)
        arrays[f"in_{name}"] = a
        args[name] = nc.dram_tensor(f"in_{name}", a.shape, mybir.dt.from_np(a.dtype), kind="ExternalInput").ap()
    args["out"] = nc.dram_tensor("out_y", (T, D), F32, kind="ExternalOutput").ap()
    hymba_kernel(nc, **args)
    r = run_bass_kernel_spmd(nc, [arrays], core_ids=[0])
    return r.results[0]["out_y"].reshape(1, T, D)
```
